# Optimizing a Trainium2 kernel written in Bass

```python
import math
import jax, jax.numpy as jnp
from jax import lax
import numpy as np

D_MODEL = 1024
BATCH = 1
SEQ = 512
DEPTH = 1

HEAD_DIM = 64
N_HEADS = D_MODEL // HEAD_DIM
MIX_WIDTH = N_HEADS * HEAD_DIM
N_HEADS_MOBA = N_HEADS // 4
N_HEADS_SB = N_HEADS // 4
N_HEADS_DIL = N_HEADS - N_HEADS_MOBA - N_HEADS_SB
MOBA_BLOCK = 256
MOBA_TOPK = 3
MOBA_QCHUNK = 32
SB_QBLOCK = 128
DIL_CONFIGS = ((128, 1), (512, 4), (2048, 16))
N_GROUPS = 4
EXPERTS_PER_GROUP = 4
MOE_TOPK = 2
D_EXPERT = D_MODEL // 4
NORM_EPS = 1e-6
NEG_INF = -1e30

kernel_name = "hymba_moba_stickbreak_dilated_hmoe"

def rms_norm(x, g):
    xf = x.astype(jnp.float32)
    y = xf * lax.rsqrt(jnp.mean(xf * xf, axis=-1, keepdims=True) + NORM_EPS)
    return (y * g.astype(jnp.float32)).astype(x.dtype)

def alibi_slopes(n):
    return jnp.asarray(2.0 ** (-8.0 * np.arange(1, n + 1, dtype=np.float32) / n), dtype=jnp.float32)

def moba_attention(q, k, v, slopes):
    B, H, S, hd = q.shape
    blk, qc = MOBA_BLOCK, MOBA_QCHUNK
    n_blk = -(-S // blk)
    s_pad = n_blk * blk
    pad = ((0, 0), (0, 0), (0, s_pad - S), (0, 0))
    q, k, v = jnp.pad(q, pad), jnp.pad(k, pad), jnp.pad(v, pad)
    k_blk = k.reshape(B, H, n_blk, blk, hd)
    v_blk = v.reshape(B, H, n_blk, blk, hd)
    k_mean = jnp.mean(k_blk.astype(jnp.float32), axis=3)
    n_sel = max(1, min(MOBA_TOPK, n_blk - 1))
    scale = hd ** -0.5
    n_chunks = s_pad // qc
    q_chunks = q.reshape(B, H, n_chunks, qc, hd).transpose(2, 0, 1, 3, 4)
    b_ix = jnp.arange(B)[:, None, None, None]
    h_ix = jnp.arange(H)[None, :, None, None]
    m = slopes[None, :, None, None]

    def chunk(args):
        q_c, c = args
        t0 = c * qc
        own = t0 // blk
        t = t0 + jnp.arange(qc)
        qf = q_c.astype(jnp.float32)
        gate = jnp.einsum('bhqd,bhnd->bhqn', qf, k_mean)
        gate = jnp.where(jnp.arange(n_blk) < own, gate, NEG_INF)
        _, sel = lax.top_k(gate, n_sel)
        sel_ok = sel < own
        k_sel = k_blk[b_ix, h_ix, sel].astype(jnp.float32)
        v_sel = v_blk[b_ix, h_ix, sel].astype(jnp.float32)
        pos_sel = sel[..., None] * blk + jnp.arange(blk)
        s_sel = jnp.einsum('bhqd,bhqnkd->bhqnk', qf, k_sel) * scale
        s_sel = s_sel - m[..., None] * (t[:, None, None] - pos_sel).astype(jnp.float32)
        s_sel = jnp.where(sel_ok[..., None], s_sel, NEG_INF).reshape(B, H, qc, n_sel * blk)
        k_own = lax.dynamic_slice_in_dim(k, own * blk, blk, axis=2).astype(jnp.float32)
        v_own = lax.dynamic_slice_in_dim(v, own * blk, blk, axis=2).astype(jnp.float32)
        dist = t[:, None] - (own * blk + jnp.arange(blk))[None, :]
        s_own = jnp.einsum('bhqd,bhkd->bhqk', qf, k_own) * scale - m * dist.astype(jnp.float32)
        s_own = jnp.where(dist >= 0, s_own, NEG_INF)
        p = jax.nn.softmax(jnp.concatenate([s_sel, s_own], axis=-1), axis=-1)
        p_sel = p[..., :n_sel * blk].reshape(B, H, qc, n_sel, blk)
        p_own = p[..., n_sel * blk:]
        o = (jnp.einsum('bhqnk,bhqnkd->bhqd', p_sel, v_sel)
             + jnp.einsum('bhqk,bhkd->bhqd', p_own, v_own))
        return o.astype(v.dtype)

    o = lax.map(chunk, (q_chunks, jnp.arange(n_chunks)))
    return o.transpose(1, 2, 0, 3, 4).reshape(B, H, s_pad, hd)[:, :, :S]

def stick_breaking_attention(q, k, v):
    B, H, S, hd = q.shape
    qb = SB_QBLOCK
    n_qb = S // qb
    scale = hd ** -0.5
    k_pos = jnp.arange(S)
    q_blocks = q.reshape(B, H, n_qb, qb, hd).transpose(2, 0, 1, 3, 4)
    kf = k.astype(jnp.float32)
    vf = v.astype(jnp.float32)

    def block(args):
        q_b, i = args
        t = i * qb + jnp.arange(qb)
        z = jnp.einsum('bhqd,bhkd->bhqk', q_b.astype(jnp.float32), kf) * scale
        past = k_pos[None, :] < t[:, None]
        log_not = jnp.where(past, jax.nn.log_sigmoid(-z), 0.0)
        tail = lax.cumsum(log_not, axis=3, reverse=True) - log_not
        a = jnp.where(past, jnp.exp(jax.nn.log_sigmoid(z) + tail), 0.0)
        return jnp.einsum('bhqk,bhkd->bhqd', a, vf).astype(v.dtype)

    o = lax.map(block, (q_blocks, jnp.arange(n_qb)))
    return o.transpose(1, 2, 0, 3, 4).reshape(B, H, S, hd)

def dilated_branch(q, k, v, slopes, window, dilation):
    B, H, S, hd = q.shape
    n = window // dilation
    L = S // dilation
    n_blk = -(-L // n)
    l_pad = n_blk * n

    def to_blocks(t):
        t = t.reshape(B, H, L, dilation, hd).transpose(0, 1, 3, 2, 4)
        t = jnp.pad(t, ((0, 0), (0, 0), (0, 0), (0, l_pad - L), (0, 0)))
        return t.reshape(B, H, dilation, n_blk, n, hd)

    def with_prev(t):
        prev = jnp.pad(t, ((0, 0), (0, 0), (0, 0), (1, 0), (0, 0), (0, 0)))[:, :, :, :-1]
        return jnp.concatenate([prev, t], axis=4)

    qb = to_blocks(q).astype(jnp.float32)
    kb = with_prev(to_blocks(k)).astype(jnp.float32)
    vb = with_prev(to_blocks(v)).astype(jnp.float32)
    delta = jnp.arange(n)[:, None] + n - jnp.arange(2 * n)[None, :]
    k_sub = jnp.arange(n_blk)[:, None] * n - n + jnp.arange(2 * n)[None, :]
    valid = ((delta >= 0) & (delta <= n))[None] & (k_sub >= 0)[:, None, :]
    s = jnp.einsum('bhrnqd,bhrnkd->bhrnqk', qb, kb) * (hd ** -0.5)
    s = s - slopes[:, None, None, None, None] * (delta * dilation).astype(jnp.float32)
    s = jnp.where(valid, s, NEG_INF)
    s_max = jnp.max(s, axis=-1, keepdims=True)
    p = jnp.exp(s - s_max)
    den = jnp.sum(p, axis=-1, keepdims=True)
    o = jnp.einsum('bhrnqk,bhrnkd->bhrnqd', p, vb) / den
    lse = (s_max + jnp.log(den))[..., 0]

    def from_blocks(t):
        t = t.reshape((B, H, dilation, l_pad) + t.shape[5:])[:, :, :, :L]
        t = jnp.moveaxis(t, 2, 3)
        return t.reshape((B, H, S) + t.shape[4:])

    return from_blocks(o), from_blocks(lse)

def dilated_mixture(q, k, v, slopes):
    outs, lses = [], []
    for window, dilation in DIL_CONFIGS:
        o, lse = dilated_branch(q, k, v, slopes, window, dilation)
        outs.append(o)
        lses.append(lse)
    wts = jax.nn.softmax(jnp.stack(lses), axis=0)
    o = jnp.einsum('cbhs,cbhsd->bhsd', wts, jnp.stack(outs))
    return o.astype(v.dtype)

def mixer_sublayer(x, ln_g, w_in, mix_g, w_out):
    B, S, _ = x.shape
    h = rms_norm(x, ln_g)
    qkv = (h @ w_in).reshape(B, S, 3, N_HEADS, HEAD_DIM).transpose(2, 0, 3, 1, 4)
    q, k, v = qkv[0], qkv[1], qkv[2]
    a = N_HEADS_MOBA
    b = N_HEADS_MOBA + N_HEADS_SB
    o_a = moba_attention(q[:, :a], k[:, :a], v[:, :a], alibi_slopes(N_HEADS_MOBA))
    o_b = stick_breaking_attention(q[:, a:b], k[:, a:b], v[:, a:b])
    o_c = dilated_mixture(q[:, b:], k[:, b:], v[:, b:], alibi_slopes(N_HEADS_DIL))

    def merge(o):
        return o.transpose(0, 2, 1, 3).reshape(B, S, -1)

    wa, wb = a * HEAD_DIM, b * HEAD_DIM
    y = jnp.concatenate([rms_norm(merge(o_a), mix_g[:wa]),
                         rms_norm(merge(o_b), mix_g[wa:wb]),
                         rms_norm(merge(o_c), mix_g[wb:])], axis=-1)
    return x + (y @ w_out).astype(x.dtype)

def hierarchical_moe(h, w_gr, b_gr, w_er, b_er, w_gate, w_up, w_down):
    f32 = jnp.float32
    hf = h.astype(f32)
    g_prob = jax.nn.softmax(hf @ w_gr.astype(f32) + b_gr.astype(f32), axis=-1)
    g_w, g_idx = lax.top_k(g_prob, 1)
    g_onehot = jax.nn.one_hot(g_idx[..., 0], N_GROUPS, dtype=f32)
    e_logits = jnp.einsum('bsd,gde->bsge', hf, w_er.astype(f32)) + b_er.astype(f32)
    e_logits = jnp.einsum('bsge,bsg->bse', e_logits, g_onehot)
    e_val, e_idx = lax.top_k(e_logits, MOE_TOPK)
    e_w = jax.nn.softmax(e_val, axis=-1) * g_w
    within = jnp.sum(jax.nn.one_hot(e_idx, EXPERTS_PER_GROUP, dtype=f32) * e_w[..., None], axis=-2)
    combine = g_onehot[..., None] * within[:, :, None, :]
    y = jnp.zeros(hf.shape, f32)
    for g in range(N_GROUPS):
        gate = jnp.einsum('bsd,edf->bsef', h, w_gate[g])
        up = jnp.einsum('bsd,edf->bsef', h, w_up[g])
        act = jax.nn.silu(gate) * up * combine[:, :, g, :, None].astype(h.dtype)
        y = y + jnp.einsum('bsef,efd->bsd', act, w_down[g]).astype(f32)
    return y.astype(h.dtype)

def setup_inputs(seed: int = 0) -> dict:
    key = jax.random.key(seed)
    ks = jax.random.split(key, 16)
    f32 = jnp.float32
    D = D_MODEL

    def nrm(k, shape, scale):
        return jax.random.normal(k, shape, f32) * scale

    return {
        "x": nrm(ks[0], (BATCH, SEQ, D), 1.0),
        "ln1_g": 1.0 + nrm(ks[1], (DEPTH, D), 0.02),
        "w_in": nrm(ks[2], (DEPTH, D, 3 * MIX_WIDTH), D ** -0.5),
        "mix_norm_g": 1.0 + nrm(ks[3], (DEPTH, MIX_WIDTH), 0.02),
        "w_out": nrm(ks[4], (DEPTH, MIX_WIDTH, D), MIX_WIDTH ** -0.5),
        "ln2_g": 1.0 + nrm(ks[5], (DEPTH, D), 0.02),
        "w_group_router": nrm(ks[6], (DEPTH, D, N_GROUPS), D ** -0.5),
        "b_group_router": nrm(ks[7], (DEPTH, N_GROUPS), 0.01),
        "w_expert_router": nrm(ks[8], (DEPTH, N_GROUPS, D, EXPERTS_PER_GROUP), D ** -0.5),
        "b_expert_router": nrm(ks[9], (DEPTH, N_GROUPS, EXPERTS_PER_GROUP), 0.01),
        "w_gate": nrm(ks[10], (DEPTH, N_GROUPS, EXPERTS_PER_GROUP, D, D_EXPERT), D ** -0.5),
        "w_up": nrm(ks[11], (DEPTH, N_GROUPS, EXPERTS_PER_GROUP, D, D_EXPERT), D ** -0.5),
        "w_down": nrm(ks[12], (DEPTH, N_GROUPS, EXPERTS_PER_GROUP, D_EXPERT, D), D_EXPERT ** -0.5),
        "final_norm_g": 1.0 + nrm(ks[13], (D,), 0.02),
    }

def reference(x, ln1_g, w_in, mix_norm_g, w_out, ln2_g, w_group_router, b_group_router,
              w_expert_router, b_expert_router, w_gate, w_up, w_down, final_norm_g):
    for l in range(DEPTH):
        x = mixer_sublayer(x, ln1_g[l], w_in[l], mix_norm_g[l], w_out[l])
        x = x + hierarchical_moe(rms_norm(x, ln2_g[l]), w_group_router[l], b_group_router[l],
                                 w_expert_router[l], b_expert_router[l],
                                 w_gate[l], w_up[l], w_down[l])
    return rms_norm(x, final_norm_g)


_drawn_inputs = setup_inputs


def setup_inputs(seed=0):
    import zlib

    import numpy as np

    out = dict(_drawn_inputs(seed))
    spreads = {}
    factors = {'mix_norm_g': 3.708,
     'ln2_g': 3.196,
     'b_group_router': 8.0,
     'b_expert_router': 7.798,
     'final_norm_g': 2.746}
    for name, (base, spread) in spreads.items():
        noise = np.random.default_rng([zlib.crc32(name.encode()), seed]).standard_normal(out[name].shape)
        drawn = base * np.exp(spread * noise) if base else spread * noise
        out[name] = __import__('jax').numpy.asarray(drawn.astype(out[name].dtype))
    for name, factor in factors.items():
        out[name] = (out[name] * factor).astype(out[name].dtype)
    return out
```

```python
import concourse.bass as bass
from concourse import mybir
from contextlib import ExitStack

P = 128
SEQ, D = 512, 1024
HEADS, HD = 16, 64
TILES = SEQ // P
KC = D // P
PAIRS = HEADS // 2
SOFT_PAIRS = 6
GROUPS, PER_GROUP = 4, 4
EXPERTS = GROUPS * PER_GROUP
DE = D // 4
RC = DE // P
ROUTES = GROUPS + EXPERTS
TOPK = 2
SLOT_TURNS = SEQ // P
EPS = 1e-6
NEG = -1e30
UNITS = 2 * TILES
SETS = 4
EXPERT_TURNS = EXPERTS // SETS
WORDS = KC * 2 * DE + RC * D
BIG = 1 << 20
SLOPES = [2.0 ** (-8.0 * (i + 1) / 4) for i in range(4)] + [2.0 ** (-8.0 * (i + 1) / 8) for i in range(8)]
MIX_GROUPS = [(0, 2), (2, 6), (6, 8)]


class Tally:

    def __init__(self, eng, sem):
        self.eng, self.sem, self.n, self.offset = eng, sem, 0, None

    def now(self):
        return self.n if self.offset is None else self.offset + self.n

    def mark(self, ins):
        ins.then_inc(self.sem, 1)
        self.n += 1
        return self.now()

    def wait(self, value=None):
        self.eng.wait_ge(self.sem, self.now() if value is None else value)

    def step(self, ins):
        self.mark(ins)
        self.wait()

    def enter(self, turn, per):
        self.first, self.per, self.offset = self.n, per, turn * per

    def leave(self, turns):
        assert self.n - self.first == self.per, (self.n - self.first, self.per)
        self.n, self.offset = self.first + turns * self.per, None


def decoder_layer(nc, x, gain1, w_qkv, gain_mix, w_out, gain2, w_route, b_route, w_expert, gain_final, out):
    F32, I32 = mybir.dt.float32, mybir.dt.int32
    U32 = mybir.dt.uint32
    ALU, ACT = mybir.AluOpType, mybir.ActivationFunctionType

    ctx = ExitStack()
    with ctx:
        def sb(name, shape, dt=F32):
            return ctx.enter_context(nc.sbuf_tensor(name, shape, dt))

        def sem(name):
            return ctx.enter_context(nc.semaphore(name))

        x_rows = sb("x_rows", [P, TILES, D])
        gain_row = sb("gain_row", [P, D])
        front = sb("front", [P, KC * SEQ + 3 * KC * P])
        hT = front[:, 0:KC * SEQ].rearrange("p (c t) -> p c t", c=KC)
        w_pair = front[:, KC * SEQ:].rearrange("p (s c m) -> p s c m", s=3, c=KC)
        set0, set1 = sb("set0", [P, WORDS]), sb("set1", [P, WORDS])
        mixer_w = sb("mixer_w", [P, PAIRS * D])
        wo = mixer_w[:, :].rearrange("p (c n) -> p c n", c=PAIRS)
        attn = sb("attn", [P, WORDS])
        sets = [set0[:, :], set1[:, :], mixer_w[:, 0:WORDS], attn[:, :]]
        o_all = sb("o_all", [P, PAIRS, SEQ])
        wide = sb("wide", [P, 2 * TILES * SEQ])

        at = [0]

        def part(region, words):
            at[0] += words
            return region[:, at[0] - words:at[0]]

        prob = part(attn, 4 * SEQ).rearrange("p (r n) -> p r n", r=4)
        qT, kT = part(attn, SEQ), part(attn, SEQ)
        v_tok = part(attn, SEQ).rearrange("p (j d) -> p j d", j=TILES)
        bias = part(attn, 2 * SEQ).rearrange("p (a n) -> p a n", a=2)
        log_count = part(attn, 2 * SEQ).rearrange("p (a n) -> p a n", a=2)
        neg_dist = part(attn, SEQ)
        assert at[0] <= WORDS
        probT = wide[:, :].rearrange("p (a j q) -> p a j q", a=2, j=TILES)
        SB_W = [SEQ - P * j for j in range(TILES)]
        SB_AT = [sum(SB_W[:j]) for j in range(TILES)]
        sb_n = sum(SB_W)
        soft = [wide[:, a * sb_n:(a + 1) * sb_n] for a in range(2)]
        stick = [wide[:, 2 * sb_n:3 * sb_n], attn[:, 0:sb_n]]
        h_rows = o_all[:, :, :].rearrange("p c t -> p (c t)").rearrange("p (t d) -> p t d", t=TILES)
        h2_rows = wide[:, :].rearrange("p (t d) -> p t d", t=TILES)
        h2T = o_all[:, :, :]
        at[0] = 0
        x_slot = part(front, 2 * D).rearrange("p (r d) -> p r d", r=2)
        xT = part(front, 2 * D).rearrange("p (r c s) -> p r c s", r=2, c=KC)
        actT = part(front, 2 * DE).rearrange("p (r c s) -> p r c s", r=2, c=RC)
        act_t = part(front, 4 * DE).rearrange("p (r f) -> p r f", r=4)
        y_slot = mixer_w[:, WORDS:].rearrange("p (r d) -> p r d", r=2)
        assert at[0] <= KC * SEQ + 3 * KC * P
        y_pairs = [set0[:, 0:2 * D], set0[:, 2 * D:4 * D], set1[:, 0:2 * D], set1[:, 2 * D:4 * D]]

        ident, ones = sb("ident", [P, P]), sb("ones", [P, P])
        neg_tri, neg_ones, before = sb("neg_tri", [P, P]), sb("neg_ones", [P, P]), sb("before", [P, P])
        slope = sb("slope", [P, 2 * SOFT_PAIRS])
        dist_i = wide[:, 0:SEQ].bitcast(I32)
        mod_i = wide[:, SEQ:2 * SEQ].bitcast(I32)
        hits, count = wide[:, 2 * SEQ:3 * SEQ], wide[:, 3 * SEQ:4 * SEQ]
        gain_m = sb("gain_m", [P, PAIRS])
        wr = sb("wr", [P, KC, ROUTES])
        br = sb("br", [1, ROUTES])
        ss = sb("ss", [P, TILES])
        var, rs, nt = sb("var", [P, TILES]), sb("rs", [P, TILES]), sb("nt", [P, TILES])
        neg_max, den, rden = sb("neg_max", [P, UNITS]), sb("den", [P, UNITS]), sb("rden", [P, UNITS])
        logits = sb("logits", [P, TILES, ROUTES])
        pad = sb("pad", [P, 2 * TILES, 8])
        top = sb("top", [P, 2 * TILES, 8])
        top_i = sb("top_i", [P, 2 * TILES, 8], U32)
        idx_f = sb("idx_f", [P, 2 * TILES, 2])
        iota16 = sb("iota16", [P, EXPERTS])
        pick = sb("pick", [P, TILES, GROUPS])
        scr = sb("scr", [P, TILES, EXPERTS])
        chosen = sb("chosen", [P, TOPK, TILES, EXPERTS])
        member = sb("member", [P, TILES, EXPERTS])
        eid = sb("eid", [P, TOPK, TILES])
        rank = sb("rank", [P, TOPK, TILES])
        turn_f = sb("turn_f", [P, TOPK, TILES])
        tmp_f = sb("tmp_f", [P, TOPK, TILES])
        row_i = sb("row_i", [P, TOPK, TILES], U32)
        token_f = sb("token_f", [P, TOPK, TILES])
        token_i = sb("token_i", [P, TOPK, TILES], I32)
        weight = sb("weight", [P, TOPK, TILES])
        gsm = sb("gsm", [P, 4, TILES])
        group_exp = sb("group_exp", [P, TILES, GROUPS])
        empty = sb("empty", [P, SLOT_TURNS * EXPERTS], I32)
        slot_to = sb("slot_to", [P, SLOT_TURNS * EXPERTS], I32)
        slot_of = sb("slot_of", [P, SLOT_TURNS * EXPERTS], I32)
        gather_at, scatter_at = sb("gather_at", [P, SETS], I32), sb("scatter_at", [P, SETS], I32)
        dve_tick, pool_tick = sb("dve_tick", [1, UNITS]), sb("pool_tick", [1, 2 * SETS])
        fullest = sb("fullest", [1, 4])
        turns_i = sb("turns_i", [1, 1], I32)

        bank = [ctx.enter_context(nc.psum_tensor(f"bank{i}", [P, 512], F32)) for i in range(8)]
        S, T, O_BANK, PQ, PK, PV = bank[0:2], bank[2:4], bank[4], bank[5], bank[6], bank[7]

        h2_dram = nc.dram_tensor("h2_dram", [SEQ, D], F32).ap()
        y_dram = nc.dram_tensor("y_dram", [SEQ * TOPK, D], F32).ap()
        empty_dram = nc.dram_tensor("empty_dram", [P, 1], I32).ap()
        table = nc.dram_tensor("slot_table", [P * SLOT_TURNS * EXPERTS, 1], I32).ap()

        x_in, gain_in, small_in = [sem(f"x_in{t}") for t in range(TILES)], sem("gain_in"), sem("small_in")
        wqk_in, wv_in, wo_in = sem("wqk_in"), sem("wv_in"), sem("wo_in")
        expert_in = [sem(f"expert_in{b}") for b in range(SETS)]
        pool_own, act_own, dve_own, end_own, act_end = (sem(n) for n in ("pool_own", "act_own", "dve_own", "end_own", "act_end"))
        consts_ready, squares_done, gain1_used = sem("consts_ready"), sem("squares_done"), sem("gain1_used")
        iota_ready, count_ready, log_ready = sem("iota_ready"), sem("count_ready"), sem("log_ready")
        rows_ready, turned, hT_ready = sem("rows_ready"), sem("turned"), sem("hT_ready")
        q_done, k_done, v_done = sem("q_done"), sem("k_done"), sem("v_done")
        qk_ready, v_ready = sem("qk_ready"), sem("v_ready")
        score_done, biased, exp_done, normed = sem("score_done"), sem("biased"), sem("exp_done"), sem("normed")
        prob_turned, probT_ready, pv_done, o_ready = sem("prob_turned"), sem("probT_ready"), sem("pv_done"), sem("o_ready")
        z_done, abs_done, ln_done, soft_ready = sem("z_done"), sem("abs_done"), sem("ln_done"), sem("soft_ready")
        stick_sum, stick_exp, stick_ready = sem("stick_sum"), sem("stick_exp"), sem("stick_ready")
        sq_ready, sq_summed, root_ready, y_ready = sem("sq_ready"), sem("sq_summed"), sem("root_ready"), sem("y_ready")
        root_in = sem("root_in")
        mixed, x1_ready, h2_ready, h2_stored = sem("mixed"), sem("x1_ready"), sem("h2_ready"), sem("h2_stored")
        turned2, h2T_ready, routed, logits_ready = sem("turned2"), sem("h2T_ready"), sem("routed"), sem("logits_ready")
        gate_in, gate_out = sem("gate_in"), sem("gate_out")
        member_ready, ranked, counted = sem("member_ready"), sem("ranked"), sem("counted")
        rows_known, table_empty, table_filled, table_in = sem("rows_known"), sem("table_empty"), sem("table_filled"), sem("table_in")
        slots_ready, turns_ready = sem("slots_ready"), sem("turns_ready")
        gathered = [sem(f"gathered{r}") for r in range(2)]
        scattered = [sem(f"scattered{r}") for r in range(2)]
        xT_done, xT_ready, gu_done, sig_ready, act_ready = sem("xT_done"), sem("xT_ready"), sem("gu_done"), sem("sig_ready"), sem("act_ready")
        actT_done, actT_ready, y_done, y0_copied, y1_copied = sem("actT_done"), sem("actT_ready"), sem("y_done"), sem("y0_copied"), sem("y1_copied")
        y_in = [sem(f"y_in{t}") for t in range(TILES)]
        x2_ready, sq2_done, out_ready, stored = sem("x2_ready"), sem("sq2_done"), sem("out_ready"), sem("stored")

        block = ctx.enter_context(nc.Block())

        @block.sync
        def _(sp):
            for t in range(TILES):
                sp.dma_start(x_rows[:, t, :], x[t * P:(t + 1) * P, :]).then_inc(x_in[t], 16)
            sp.dma_start(gain_row[:, :], gain1.partition_broadcast(P)).then_inc(gain_in, 16)

            def load_qk(n):
                sp.dma_start(w_pair[:, 0:2, :, :], w_qkv[n, :, 0:2 * KC * P]
                             .rearrange("p (s c m) -> p s c m", s=2, c=KC)).then_inc(wqk_in, 16)

            def load_v(n):
                sp.dma_start(w_pair[:, 2, :, :], w_qkv[n, :, 2 * KC * P:3 * KC * P]
                             .rearrange("p (c m) -> p c m", c=KC)).then_inc(wv_in, 16)

            load_qk(0)
            load_v(0)
            sp.dma_start(gain_m[:, :], gain_mix).then_inc(small_in, 16)
            sp.dma_start(wr[:, :, :], w_route.rearrange("p (c n) -> p c n", c=KC)).then_inc(small_in, 16)
            sp.dma_start(br[:, :], b_route).then_inc(small_in, 16)
            sp.dma_start(wo, w_out.rearrange("p (c n) -> p c n", c=PAIRS)).then_inc(wo_in, 16)
            sp.wait_ge(consts_ready, 1)
            sp.dma_start(empty_dram, empty[:, 0:1]).then_inc(table_empty, 16)
            sp.dma_start(table.rearrange("(p n) a -> p (n a)", p=P), empty[:, :]).then_inc(table_empty, 16)
            sp.wait_ge(rows_ready, TILES)
            sp.dma_start(gain_row[:, :], gain2.partition_broadcast(P)).then_inc(gain_in, 16)
            sp.wait_ge(k_done, 1)
            load_qk(1)
            sp.wait_ge(v_done, 1)
            load_v(1)
            for b in range(2):
                sp.dma_start(sets[b], w_expert[b]).then_inc(expert_in[b], 16)
            with sp.Fori(2, PAIRS) as n:
                sp.wait_ge(k_done, n)
                load_qk(n)
                sp.wait_ge(v_done, n)
                load_v(n)

            sp.wait_ge(mixed, TILES * 2)
            sp.dma_start(sets[2], w_expert[2]).then_inc(expert_in[2], 16)
            sp.dma_start(sets[3], w_expert[3]).then_inc(expert_in[3], 16)
            for t in range(TILES):
                sp.wait_ge(h2_ready, t + 1)
                sp.dma_start(h2_dram[t * P:(t + 1) * P, :], h2_rows[:, t, :]).then_inc(h2_stored, 16)
            sp.wait_ge(h2_ready, TILES)
            sp.dma_start(gain_row[:, :], gain_final.partition_broadcast(P)).then_inc(gain_in, 16)
            sp.wait_ge(table_filled, 16 * TOPK * TILES)
            sp.dma_start(slot_to[:, :], table.rearrange("(p n) a -> p (n a)", p=P)).then_inc(table_in, 16)

            sp.wait_ge(turns_ready, 1)
            turns = sp.value_load(turns_i[0:1, 0:1], min_val=EXPERT_TURNS, max_val=EXPERT_TURNS * SLOT_TURNS)
            with sp.Fori(1, turns) as it:
                for b in range(SETS):
                    sp.wait_ge(y_done, it * (2 * SETS) + (2 * b + 2 - 2 * SETS))
                    sp.dma_start(sets[b], w_expert[(it % EXPERT_TURNS) * SETS + b, :, :]).then_inc(expert_in[b], 16)

            for r in range(2):
                sp.wait_ge(scattered[r], turns * (16 * SETS // 2) + 16)
            for t in range(TILES):
                sp.dma_start(y_pairs[t], y_dram[t * P * TOPK:(t + 1) * P * TOPK, :]
                             .rearrange("(p k) d -> p (k d)", k=TOPK)).then_inc(y_in[t], 16)
            for t in range(TILES):
                sp.wait_ge(out_ready, t + 1)
                sp.dma_start(out[t * P:(t + 1) * P, :], h2_rows[:, t, :]).then_inc(stored, 16)
            sp.wait_ge(stored, 16 * TILES)
            sp.wait_ge(h2_stored, 16 * TILES)

        @block.gpsimd
        def _(pool):
            own = Tally(pool, pool_own)
            pool.memset(ident[:, :], 0.0).then_inc(pool_own, 1)
            pool.memset(neg_tri[:, :], -1.0).then_inc(pool_own, 1)
            pool.memset(before[:, :], 1.0).then_inc(pool_own, 1)
            own.n = 3
            own.wait()
            own.mark(pool.affine_select(out=ident[:, :], in_=ident[:, :], compare_op=ALU.not_equal, fill=1.0,
                                        base=0, pattern=[[-1, P]], channel_multiplier=1))
            own.mark(pool.affine_select(out=neg_tri[:, :], in_=neg_tri[:, :], compare_op=ALU.is_ge, fill=0.0,
                                        base=0, pattern=[[-1, P]], channel_multiplier=1))
            own.mark(pool.affine_select(out=before[:, :], in_=before[:, :], compare_op=ALU.is_gt, fill=0.0,
                                        base=0, pattern=[[1, P]], channel_multiplier=-1))
            own.mark(pool.memset(ones[:, :], 1.0))
            own.mark(pool.memset(neg_ones[:, :], -1.0))
            own.wait()
            pool.memset(empty[:, :], BIG).then_inc(consts_ready, 1)
            pool.iota(dist_i, pattern=[[-1, SEQ]], base=SEQ - P, channel_multiplier=1).then_inc(iota_ready, 1)
            pool.iota(neg_dist, pattern=[[1, SEQ]], base=P - SEQ, channel_multiplier=-1,
                      allow_small_or_imprecise_dtypes=True).then_inc(iota_ready, 1)
            pool.iota(iota16[:, :], pattern=[[1, EXPERTS]], base=0, channel_multiplier=0,
                      allow_small_or_imprecise_dtypes=True).then_inc(iota_ready, 1)
            pool.iota(token_f[:, :, :], pattern=[[1, TOPK], [TOPK * P, TILES]], base=0, channel_multiplier=TOPK,
                      allow_small_or_imprecise_dtypes=True).then_inc(iota_ready, 1)
            for h, s in enumerate(SLOPES):
                pool.memset(slope[:, h:h + 1], s).then_inc(iota_ready, 1)
            own.mark(pool.memset(log_count[:, 0, :], 0.0))
            own.wait()
            pool.wait_ge(log_ready, 1)
            for m in range(2):
                pool.affine_select(out=log_count[:, m, :], in_=log_count[:, m, :], compare_op=ALU.is_ge, fill=NEG,
                                   base=SEQ - P, pattern=[[-1, SEQ]], channel_multiplier=1).then_inc(log_ready, 1)
            pool.memset(pad[:, :, :], NEG).then_inc(consts_ready, 1)

            for g in range(2 * (PAIRS - SOFT_PAIRS)):
                for j in reversed(range(TILES)):
                    pool.wait_ge(stick_exp, g * TILES + TILES - j)
                    tile = stick[g % 2][:, SB_AT[j]:SB_AT[j] + P]
                    pool.affine_select(out=tile, in_=tile, compare_op=ALU.is_gt, fill=0.0,
                                       base=0, pattern=[[1, P]], channel_multiplier=-1).then_inc(stick_ready, 1)

            pool.wait_ge(table_empty, 32)
            pool.wait_ge(rows_known, 1)
            for t in range(TILES):
                for k in range(TOPK):
                    pool.indirect_dma_start(out=table, out_offset=bass.IndirectOffsetOnAxis(ap=row_i[:, k, t:t + 1], axis=0),
                                            in_=token_i[:, k, t:t + 1], in_offset=None,
                                            bounds_check=P * SLOT_TURNS * EXPERTS - 1, oob_is_err=False).then_inc(table_filled, 16)
            pool.wait_ge(h2_stored, 16 * TILES)
            for r in range(2):
                pool.dma_start(x_slot[:, r, :], h2_dram[0:P, :]).then_inc(gathered[r], 16)
                pool.dma_start(scatter_at[:, r:r + 1], empty_dram).then_inc(scattered[r], 16)
            pool.wait_ge(turns_ready, 1)
            pool.wait_ge(slots_ready, 1)
            turns = pool.value_load(turns_i[0:1, 0:1], min_val=EXPERT_TURNS, max_val=EXPERT_TURNS * SLOT_TURNS)
            last_token, last_row = pool.to_reg(SEQ - 1), pool.to_reg(SEQ * TOPK - 1)
            with pool.Fori(0, turns) as it:
                own.enter(it, 2 * SETS)

                def gather(b):
                    r = b % 2
                    if b < 2:
                        pool.wait_ge(gathered[r], it * (16 * SETS // 2) + 16)
                    if b >= 2:
                        pool.wait_ge(xT_done, it * SETS + (b - 1))
                    own.step(pool.tensor_copy(gather_at[:, b:b + 1], slot_of[:, bass.ds(it * SETS + b, 1)]))
                    pool.tensor_tensor(pool_tick[:, b:b + 1], ones[0:1, 0:1], ones[0:1, 0:1], ALU.add)
                    pool.indirect_dma_start(out=x_slot[:, r, :], out_offset=None, in_=h2_dram,
                                            in_offset=bass.IndirectOffsetOnAxis(ap=gather_at[:, b:b + 1].bitcast(U32), axis=0),
                                            bounds_check=last_token, oob_is_err=False).then_inc(gathered[r], 16)

                def scatter(b):
                    r = b % 2
                    pool.wait_ge(scattered[r], it * (16 * SETS // 2) + 16)
                    own.step(pool.tensor_copy(scatter_at[:, b:b + 1], slot_to[:, bass.ds(it * SETS + b, 1)]))
                    pool.wait_ge(y0_copied, it * SETS + b + 2)
                    pool.wait_ge(y1_copied, it * SETS + b + 2)
                    pool.tensor_tensor(pool_tick[:, SETS + b:SETS + b + 1], ones[0:1, 0:1], ones[0:1, 0:1], ALU.add)
                    pool.indirect_dma_start(out=y_dram, out_offset=bass.IndirectOffsetOnAxis(ap=scatter_at[:, b:b + 1].bitcast(U32), axis=0),
                                            in_=y_slot[:, r, :], in_offset=None,
                                            bounds_check=last_row, oob_is_err=False).then_inc(scattered[r], 16)

                for b in range(SETS):
                    gather(b)
                for b in range(SETS):
                    scatter(b)

        @block.tensor
        def _(pe):
            pe.wait_ge(consts_ready, 1)
            pe.wait_ge(rows_ready, TILES)
            for c in range(KC):
                if c >= 2:
                    pe.wait_ge(hT_ready, c - 1)
                for t in range(TILES):
                    mm = pe.transpose(S[c % 2][:, t * P:(t + 1) * P], h_rows[:, t, c * P:(c + 1) * P], ident[:, :])
                mm.then_inc(turned, 1)

            def project_T(dst, s, done):
                for c in range(KC):
                    mm = pe.matmul(dst[:, :], w_pair[:, s, c, :], hT[:, c, :], start=(c == 0), stop=(c == KC - 1))
                mm.then_inc(done, 1)

            def project_v(n):
                pe.wait_ge(wv_in, n * 16 + 16)
                for t in range(TILES):
                    for c in range(KC):
                        mm = pe.matmul(PV[:, t * P:(t + 1) * P], hT[:, c, t * P:(t + 1) * P], w_pair[:, 2, c, :],
                                       start=(c == 0), stop=(c == KC - 1))
                mm.then_inc(v_done, 1)

            pe.wait_ge(hT_ready, KC)
            pe.wait_ge(wqk_in, 16)
            project_T(PQ, 0, q_done)
            project_T(PK, 1, k_done)

            def scores(n, u):
                a, i = divmod(u, TILES)
                w = (i + 1) * P
                if u >= 2:
                    pe.wait_ge(biased, n * UNITS + (u - 1))
                h = slice(a * HD, (a + 1) * HD)
                pe.matmul(S[u % 2][:, 0:w], qT[h, i * P:w], kT[h, 0:w], start=True, stop=True).then_inc(score_done, 1)

            def turn(n, u):
                a, i = divmod(u, TILES)
                pe.wait_ge(normed, n * UNITS + (u + 1))
                if u >= 2:
                    pe.wait_ge(probT_ready, n * UNITS + (u - 1))
                for j in range(i + 1):
                    mm = pe.transpose(T[u % 2][:, j * P:(j + 1) * P], prob[:, u % 4, j * P:(j + 1) * P], ident[:, :])
                mm.then_inc(prob_turned, 1)

            def values(n, a, src, ready):
                ready()
                pe.wait_ge(v_ready, n + 1)
                if a == 0:
                    pe.wait_ge(o_ready, n + 1)
                for j in range(TILES):
                    mm = pe.matmul(O_BANK[a * HD:(a + 1) * HD, j * P:SEQ], v_tok[:, j, a * HD:(a + 1) * HD], src(j),
                                   start=(j == 0), stop=(j == TILES - 1), skip_group_check=True)
                mm.then_inc(pv_done, 1)

            with pe.Fori(0, SOFT_PAIRS) as n:
                pe.wait_ge(qk_ready, 2 * n + 2)
                for u in range(UNITS):
                    scores(n, u)
                    if u == 1:
                        project_v(n)
                    if u >= 2:
                        turn(n, u - 2)
                    if u == 6:
                        values(n, 0, lambda j: probT[:, 0, j, j * P:SEQ],
                               lambda: pe.wait_ge(probT_ready, n * UNITS + TILES))
                pe.wait_ge(wqk_in, 16 * n + 32)
                project_T(PQ, 0, q_done)
                turn(n, UNITS - 2)
                project_T(PK, 1, k_done)
                turn(n, UNITS - 1)
                values(n, 1, lambda j: probT[:, 1, j, j * P:SEQ],
                       lambda: pe.wait_ge(probT_ready, n * UNITS + UNITS))

            Z = bank[0:4]

            def stick_z(n, a):
                g = 2 * (n - SOFT_PAIRS) + a
                h = slice(a * HD, (a + 1) * HD)
                for j in reversed(range(TILES)):
                    if g >= 1:
                        pe.wait_ge(stick_exp, (g - 1) * TILES + TILES - j)
                    pe.matmul(Z[j][:, 0:SB_W[j]], kT[h, j * P:(j + 1) * P], qT[h, j * P:SEQ], start=True, stop=False,
                              skip_group_check=True).then_inc(z_done, 1)

            def stick_tail(n, a):
                g = 2 * (n - SOFT_PAIRS) + a
                for j in reversed(range(TILES)):
                    pe.wait_ge(soft_ready, g * TILES + TILES - j)
                    for jj in reversed(range(j, TILES)):
                        mm = pe.matmul(Z[j][:, (jj - j) * P:SB_W[j]], (neg_tri if jj == j else neg_ones)[:, :],
                                       soft[a][:, SB_AT[jj]:SB_AT[jj] + SB_W[jj]], start=False, stop=(jj == j),
                                       skip_group_check=True)
                    mm.then_inc(stick_sum, 1)

            for n in range(SOFT_PAIRS, PAIRS):
                g = 2 * (n - SOFT_PAIRS)
                pe.wait_ge(qk_ready, 2 * n + 2)
                stick_z(n, 0)
                project_v(n)
                stick_tail(n, 0)
                stick_z(n, 1)
                if n + 1 < PAIRS:
                    pe.wait_ge(wqk_in, 16 * (n + 2))
                    project_T(PQ, 0, q_done)
                    project_T(PK, 1, k_done)
                for a in range(2):
                    if a == 1:
                        stick_tail(n, 1)
                    values(n, a, lambda j, a=a: stick[a][:, SB_AT[j]:SB_AT[j] + SB_W[j]],
                           lambda a=a, g=g: pe.wait_ge(stick_ready, (g + a + 1) * TILES))

            for g, (lo, hi) in enumerate(MIX_GROUPS):
                for n in range(lo, hi):
                    pe.wait_ge(sq_ready, n + 1)
                    mm = pe.matmul(bank[g][:, :], ones[:, :], probT[:, n // TILES, n % TILES, :], start=(n == lo), stop=(n == hi - 1))
                mm.then_inc(sq_summed, 1)

            pe.wait_ge(wo_in, 16)
            pe.wait_ge(y_ready, PAIRS)
            for t in range(TILES):
                for half in range(2):
                    m = 2 * t + half
                    if m >= 2:
                        pe.wait_ge(x1_ready, m - 1)
                    for n in range(PAIRS):
                        mm = pe.matmul(bank[4 + m % 2][:, :], o_all[:, n, t * P:(t + 1) * P], wo[:, n, half * 512:(half + 1) * 512],
                                       start=(n == 0), stop=(n == PAIRS - 1))
                    mm.then_inc(mixed, 1)

            pe.wait_ge(h2_ready, TILES)
            for c in range(KC):
                if c >= 2:
                    pe.wait_ge(h2T_ready, c - 1)
                for t in range(TILES):
                    mm = pe.transpose(S[c % 2][:, t * P:(t + 1) * P], h2_rows[:, t, c * P:(c + 1) * P], ident[:, :])
                mm.then_inc(turned2, 1)
            pe.wait_ge(h2T_ready, KC)
            pe.wait_ge(small_in, 48)
            for t in range(TILES):
                o = bank[2][:, t * ROUTES:(t + 1) * ROUTES]
                pe.matmul(o, ones[0:1, :], br[:, :], start=True, stop=False)
                for c in range(KC):
                    mm = pe.matmul(o, h2T[:, c, t * P:(t + 1) * P], wr[:, c, :], start=False, stop=(c == KC - 1))
            mm.then_inc(routed, 1)

            pe.wait_ge(member_ready, 1)
            for t in range(TILES):
                for s in range(t + 1):
                    mm = pe.matmul(bank[3][:, t * EXPERTS:(t + 1) * EXPERTS], (before if s == t else ones)[:, :], member[:, s, :],
                                   start=(s == 0), stop=(s == t))
            mm.then_inc(ranked, 1)
            for t in range(TILES):
                mm = pe.matmul(bank[4][0:1, 0:EXPERTS], ones[:, 0:1], member[:, t, :], start=(t == 0), stop=(t == TILES - 1))
            mm.then_inc(counted, 1)

            XT, GU, AT, Y = bank[0:2], bank[2:4], bank[4], bank[5:7]
            pe.wait_ge(turns_ready, 1)
            turns = pe.value_load(turns_i[0:1, 0:1], min_val=EXPERT_TURNS, max_val=EXPERT_TURNS * SLOT_TURNS)
            with pe.Fori(0, turns) as it:
                def turn_rows(b):
                    r = b % 2
                    pe.wait_ge(gathered[r], it * (16 * SETS // 2) + 16 * (b // 2 + 2))
                    for c in range(KC):
                        if c % 4 == 0 and b:
                            pe.wait_ge(xT_ready, it * (2 * SETS) + 2 * b - 1 + c // 4)
                        mm = pe.transpose(XT[c // 4][:, (c % 4) * P:(c % 4 + 1) * P], x_slot[:, r, c * P:(c + 1) * P], ident[:, :])
                    mm.then_inc(xT_done, 1)

                def gate_up(b, half):
                    w = sets[b][:, 0:KC * 2 * DE].rearrange("p (c f) -> p c f", c=KC)
                    if half == 0:
                        pe.wait_ge(expert_in[b], it * 16 + 16)
                        if b >= 2:
                            pe.wait_ge(act_ready, it * SETS + b - 1)
                    pe.wait_ge(xT_ready, it * (2 * SETS) + 2 * b + half + 1)
                    for c in range(half * 4, half * 4 + 4):
                        mm = pe.matmul(GU[b % 2][:, :], xT[:, b % 2, c, :], w[:, c, :], start=(c == 0), stop=(c == KC - 1))
                    if half:
                        mm.then_inc(gu_done, 1)

                def turn_act(b):
                    pe.wait_ge(act_ready, it * SETS + b + 1)
                    if b:
                        pe.wait_ge(actT_ready, it * SETS + b)
                    for c in range(RC):
                        mm = pe.transpose(AT[:, c * P:(c + 1) * P], act_t[:, 3, c * P:(c + 1) * P], ident[:, :])
                    mm.then_inc(actT_done, 1)

                def down(b):
                    w = sets[b][:, KC * 2 * DE:].rearrange("p (c d) -> p c d", c=RC)
                    pe.wait_ge(actT_ready, it * SETS + b + 1)
                    for half in range(2):
                        pe.wait_ge((y0_copied, y1_copied)[half], it * SETS + b + 1)
                        for c in range(RC):
                            mm = pe.matmul(Y[half][:, :], actT[:, b % 2, c, :], w[:, c, half * 512:(half + 1) * 512],
                                           start=(c == 0), stop=(c == RC - 1))
                        mm.then_inc(y_done, 1)

                turn_rows(0)
                for b in range(SETS):
                    gate_up(b, 0)
                    if b:
                        turn_act(b - 1)
                    gate_up(b, 1)
                    if b + 1 < SETS:
                        turn_rows(b + 1)
                    if b:
                        down(b - 1)
                turn_act(SETS - 1)
                down(SETS - 1)

        @block.scalar
        def _(act):
            own = Tally(act, act_own)
            act.preload_act_table_set("natural_log_exp_and_others")

            def root(v, r, wait, done):
                wait()
                own.step(act.activation(r, v, ACT.Ln))
                act.activation(r, r, ACT.Exp, scale=-0.5).then_inc(done, 1)

            for t in range(TILES):
                act.wait_ge(x_in[t], 16)
                act.activation(h_rows[:, t, :], x_rows[:, t, :], ACT.Square, accum_out=ss[:, t:t + 1]).then_inc(squares_done, 1)
            root(var[:, :], rs[:, :], lambda: act.wait_ge(root_in, 1), root_ready)

            def copy_T(c, dst, done, came):
                act.wait_ge(came, c + 1)
                act.activation(dst, S[c % 2][:, :], ACT.Copy).then_inc(done, 1)

            for c in range(KC):
                copy_T(c, hT[:, c, :], hT_ready, turned)
            act.wait_ge(count_ready, 1)
            act.activation(log_count[:, 1, :], count, ACT.Ln).then_inc(count_ready, 1)

            def evac_q(n):
                act.wait_ge(q_done, n + 1)
                act.activation(qT, PQ[:, :], ACT.Copy, scale=HD ** -0.5).then_inc(qk_ready, 1)

            def evac_k(n):
                act.wait_ge(k_done, n + 1)
                act.activation(kT, PK[:, :], ACT.Copy).then_inc(qk_ready, 1)

            evac_q(0)
            evac_k(0)

            def exponent(n, u):
                a, i = divmod(u, TILES)
                w = (i + 1) * P
                act.wait_ge(biased, n * UNITS + (u + 1))
                act.activation(prob[:, u % 4, 0:w], prob[:, u % 4, 0:w], ACT.Exp, bias=neg_max[:, u:u + 1], scale=-1.0,
                               accum_out=den[:, u:u + 1]).then_inc(exp_done, 1)

            def store_T(n, u):
                a, i = divmod(u, TILES)
                act.wait_ge(prob_turned, n * UNITS + (u + 1))
                act.activation(probT[:, a, 0:i + 1, i * P:(i + 1) * P],
                               T[u % 2][:, 0:(i + 1) * P].rearrange("p (j q) -> p j q", q=P), ACT.Copy).then_inc(probT_ready, 1)

            with act.Fori(0, SOFT_PAIRS) as n:
                for u in range(UNITS):
                    exponent(n, u)
                    if u >= 2:
                        store_T(n, u - 2)
                evac_q(n + 1)
                store_T(n, UNITS - 2)
                evac_k(n + 1)
                store_T(n, UNITS - 1)

            for n in range(SOFT_PAIRS, PAIRS):
                for a in range(2):
                    g = 2 * (n - SOFT_PAIRS) + a
                    for j in reversed(range(TILES)):
                        cols = stick[a][:, SB_AT[j]:SB_AT[j] + SB_W[j]]
                        act.wait_ge(z_done, g * TILES + TILES - j)
                        if g >= 2:
                            act.wait_ge(pv_done, 2 * SOFT_PAIRS + g - 1)
                        own.step(act.activation(cols, bank[j][:, 0:SB_W[j]], ACT.Abs))
                        own.step(act.activation(cols, cols, ACT.Exp, scale=-1.0))
                        act.activation(cols, cols, ACT.Ln, bias=1.0).then_inc(ln_done, 1)
                    for j in reversed(range(TILES)):
                        cols = stick[a][:, SB_AT[j]:SB_AT[j] + SB_W[j]]
                        act.wait_ge(stick_sum, g * TILES + TILES - j)
                        act.activation(cols, bank[j][:, 0:SB_W[j]], ACT.Exp).then_inc(stick_exp, 1)
                    if a == 1 and n + 1 < PAIRS:
                        evac_q(n + 1)
                        evac_k(n + 1)

            for n in range(PAIRS):
                act.wait_ge(o_ready, n + 2)
                if n == 0:
                    act.wait_ge(pv_done, 2 * PAIRS)
                act.activation(probT[:, n // TILES, n % TILES, :], o_all[:, n, :], ACT.Square).then_inc(sq_ready, 1)
            for g in range(3):
                root((kT, qT, bias[:, 0, :])[g], prob[:, g, :],
                     lambda g=g: act.wait_ge(root_in, 2 + g), root_ready)

            for t in range(TILES):
                act.wait_ge(x1_ready, 2 * t + 2)
                act.activation(h2_rows[:, t, :], x_rows[:, t, :], ACT.Square, accum_out=ss[:, t:t + 1]).then_inc(squares_done, 1)
                root(var[:, t:t + 1], rs[:, t:t + 1], lambda: act.wait_ge(root_in, 5 + t), root_ready)
            for c in range(KC):
                copy_T(c, h2T[:, c, :], h2T_ready, turned2)

            act.wait_ge(gate_in, 1)
            for t in range(TILES):
                act.activation(group_exp[:, t, :], logits[:, t, 0:GROUPS], ACT.Exp, bias=gsm[:, 0, t:t + 1],
                               accum_out=gsm[:, 1, t:t + 1]).then_inc(gate_out, 1)
            act.wait_ge(gate_in, 2)
            act.activation(gsm[:, 2, :], gsm[:, 0, :], ACT.Exp).then_inc(gate_out, 1)

            act.wait_ge(turns_ready, 1)
            turns = act.value_load(turns_i[0:1, 0:1], min_val=EXPERT_TURNS, max_val=EXPERT_TURNS * SLOT_TURNS)
            act.sem_inc(y0_copied, 1)
            with act.Fori(0, turns) as it:
                def evac_xT(b):
                    act.wait_ge(xT_done, it * SETS + b + 1)
                    for half in range(2):
                        act.activation(xT[:, b % 2, 4 * half:4 * half + 4, :],
                                       bank[half][:, :].rearrange("p (c s) -> p c s", c=4), ACT.Copy).then_inc(xT_ready, 1)

                def silu_exp(b):
                    act.wait_ge(gu_done, it * SETS + b + 1)
                    if b:
                        act.wait_ge(act_ready, it * SETS + b)
                    act.activation(act_t[:, 0, :], bank[2 + b % 2][:, 0:DE], ACT.Exp, scale=-1.0).then_inc(sig_ready, 1)

                def evac_actT(b):
                    act.wait_ge(actT_done, it * SETS + b + 1)
                    act.activation(actT[:, b % 2, :, :], bank[4][:, 0:DE].rearrange("p (c s) -> p c s", c=RC),
                                   ACT.Copy).then_inc(actT_ready, 1)

                def evac_y0(b):
                    act.wait_ge(y_done, it * (2 * SETS) + 2 * b + 1)
                    act.wait_ge(scattered[b % 2], it * (16 * SETS // 2) + 16 * (b // 2 + 1))
                    act.activation(y_slot[:, b % 2, 0:512], bank[5][:, :], ACT.Copy).then_inc(y0_copied, 1)

                evac_xT(0)
                for b in range(SETS):
                    if b:
                        evac_actT(b - 1)
                    silu_exp(b)
                    if b + 1 < SETS:
                        evac_xT(b + 1)
                    if b:
                        evac_y0(b - 1)
                evac_actT(SETS - 1)
                evac_y0(SETS - 1)

            own = Tally(act, act_end)
            for t in range(TILES):
                act.wait_ge(x2_ready, TOPK * (t + 1))
                act.activation(h2_rows[:, t, :], x_rows[:, t, :], ACT.Square, accum_out=ss[:, t:t + 1]).then_inc(sq2_done, 1)
                root(var[:, t:t + 1], rs[:, t:t + 1], lambda: act.wait_ge(root_in, 9 + t), root_ready)

        @block.vector
        def _(dve):
            own = Tally(dve, dve_own)
            roots = [0]

            def variance(v, total, n):
                dve.tensor_scalar(v, total, 1.0 / n, EPS, ALU.mult, ALU.add).then_inc(root_in, 1)

            def refine(v, r, tmp):
                roots[0] += 1
                dve.wait_ge(root_ready, roots[0])
                own.step(dve.tensor_tensor(tmp, r, r, ALU.mult))
                own.step(dve.tensor_tensor(tmp, tmp, v, ALU.mult))
                own.step(dve.tensor_scalar(tmp, tmp, -0.5, 1.5, ALU.mult, ALU.add))
                own.step(dve.tensor_tensor(r, r, tmp, ALU.mult))

            dve.wait_ge(squares_done, TILES)
            variance(var[:, :], ss[:, :], D)
            dve.wait_ge(root_in, 1)
            refine(var[:, :], rs[:, :], nt[:, :])
            dve.wait_ge(gain_in, 16)
            for t in range(TILES):
                dve.scalar_tensor_tensor(out=h_rows[:, t, :], in0=x_rows[:, t, :], scalar=rs[:, t:t + 1], in1=gain_row[:, :],
                                         op0=ALU.mult, op1=ALU.mult).then_inc(rows_ready, 1)
            dve.wait_ge(iota_ready, 4 + len(SLOPES))
            own.step(dve.tensor_scalar(count, neg_dist, float(-P), None, ALU.is_ge))
            for dilation in (4, 16):
                own.step(dve.tensor_scalar(mod_i, dist_i, dilation - 1, None, ALU.bitwise_and))
                own.step(dve.scalar_tensor_tensor(out=count, in0=mod_i, scalar=0.0, in1=count, op0=ALU.is_equal, op1=ALU.add))
            own.step(dve.tensor_scalar(hits, count, 0.0, NEG, ALU.is_equal, ALU.mult))
            dve.tensor_scalar(count, count, 1.0, None, ALU.max).then_inc(count_ready, 1)
            own.step(dve.tensor_copy(token_i[:, :, :], token_f[:, :, :]))
            dve.wait_ge(count_ready, 2)
            dve.tensor_tensor(log_count[:, 1, :], log_count[:, 1, :], hits, ALU.add).then_inc(log_ready, 1)
            dve.wait_ge(log_ready, 3)
            dve.sem_inc(o_ready, 1)

            def evac_v(n):
                dve.wait_ge(v_done, n + 1)
                dve.tensor_copy(v_tok[:, :, :], PV[:, :].rearrange("p (j d) -> p j d", j=TILES)).then_inc(v_ready, 1)

            def bias_scores(n, u):
                a, i = divmod(u, TILES)
                w = (i + 1) * P
                dve.wait_ge(score_done, n * UNITS + (u + 1))
                dve.memset(dve_tick[:, u:u + 1], 0.0)
                dve.tensor_tensor_reduce(out=prob[:, u % 4, 0:w], in0=S[u % 2][:, 0:w], in1=bias[:, a, SEQ - w:SEQ],
                                         scale=-1.0, scalar=3e38, op0=ALU.add, op1=ALU.min,
                                         accum_out=neg_max[:, u:u + 1]).then_inc(biased, 1)

            def normalise(n, u):
                a, i = divmod(u, TILES)
                w = (i + 1) * P
                dve.wait_ge(exp_done, n * UNITS + (u + 1))
                own.step(dve.reciprocal(rden[:, u:u + 1], den[:, u:u + 1]))
                dve.tensor_scalar(prob[:, u % 4, 0:w], prob[:, u % 4, 0:w], rden[:, u:u + 1], None, ALU.mult).then_inc(normed, 1)

            def evac_o(n):
                dve.wait_ge(pv_done, 2 * n + 2)
                if isinstance(n, int):
                    dst = o_all[:, n, :]
                else:
                    dst = o_all[:, bass.ds(n, 1), :].rearrange("p a t -> p (a t)")
                dve.tensor_copy(dst, O_BANK[:, :]).then_inc(o_ready, 1)

            with dve.Fori(0, SOFT_PAIRS) as n:
                own.enter(n, 2 + UNITS)
                for a in range(2):
                    own.mark(dve.scalar_tensor_tensor(
                        out=bias[:, a, :], in0=neg_dist, scalar=slope[:, bass.ds(2 * n + a, 1)],
                        in1=log_count[:, bass.ds((n + 2) // 4, 1), :].rearrange("p a t -> p (a t)"),
                        op0=ALU.mult, op1=ALU.add))
                own.wait()
                for u in range(UNITS):
                    bias_scores(n, u)
                    if u == 2:
                        evac_v(n)
                    if u >= 1:
                        normalise(n, u - 1)
                normalise(n, UNITS - 1)
                evac_o(n)
            own.leave(SOFT_PAIRS)

            for n in range(SOFT_PAIRS, PAIRS):
                for a in range(2):
                    g = 2 * (n - SOFT_PAIRS) + a
                    for j in reversed(range(TILES)):
                        cols = slice(SB_AT[j], SB_AT[j] + SB_W[j])
                        dve.wait_ge(ln_done, g * TILES + TILES - j)
                        own.step(dve.scalar_tensor_tensor(out=soft[a][:, cols], in0=bank[j][:, 0:SB_W[j]], scalar=0.0,
                                                          in1=stick[a][:, cols], op0=ALU.max, op1=ALU.add))
                        diag = soft[a][:, SB_AT[j]:SB_AT[j] + P]
                        dve.tensor_tensor(diag, diag, before[:, :], ALU.mult).then_inc(soft_ready, 1)
                    if a == 0:
                        evac_v(n)
                evac_o(n)

            dve.wait_ge(small_in, 48)
            for g, (lo, hi) in enumerate(MIX_GROUPS):
                v = (kT, qT, bias[:, 0, :])[g]
                dve.wait_ge(sq_summed, g + 1)
                variance(v, bank[g][:, :], (hi - lo) * P)
                dve.wait_ge(root_in, 2 + g)
                refine(v, prob[:, g, :], bias[:, 1, :])
                for n in range(lo, hi):
                    dve.scalar_tensor_tensor(out=o_all[:, n, :], in0=o_all[:, n, :], scalar=gain_m[:, n:n + 1],
                                             in1=prob[:, g, :], op0=ALU.mult, op1=ALU.mult).then_inc(y_ready, 1)

            for t in range(TILES):
                for half in range(2):
                    cols = x_rows[:, t, half * 512:(half + 1) * 512]
                    dve.wait_ge(mixed, 2 * t + half + 1)
                    dve.tensor_tensor(cols, bank[4 + half][:, :], cols, ALU.add).then_inc(x1_ready, 1)
                dve.wait_ge(squares_done, TILES + t + 1)
                variance(var[:, t:t + 1], ss[:, t:t + 1], D)
                dve.wait_ge(root_in, 5 + t)
                refine(var[:, t:t + 1], rs[:, t:t + 1], nt[:, t:t + 1])
                dve.wait_ge(gain_in, 32)
                dve.scalar_tensor_tensor(out=h2_rows[:, t, :], in0=x_rows[:, t, :], scalar=rs[:, t:t + 1], in1=gain_row[:, :],
                                         op0=ALU.mult, op1=ALU.mult).then_inc(h2_ready, 1)

            def best(lo):
                for t in range(lo, lo + TILES):
                    own.mark(dve.max(out=top[:, t, :], in_=pad[:, t, :]))
                own.wait()
                for t in range(lo, lo + TILES):
                    own.mark(dve.max_index(out=top_i[:, t, :], in_max=top[:, t, :], in_values=pad[:, t, :]))
                own.wait()
                own.step(dve.tensor_copy(idx_f[:, lo:lo + TILES, :], top_i[:, lo:lo + TILES, 0:2]))

            dve.wait_ge(routed, 1)
            dve.wait_ge(consts_ready, 2)
            own.mark(dve.tensor_copy(logits[:, :, :], bank[2][:, 0:TILES * ROUTES].rearrange("p (t n) -> p t n", t=TILES)))
            own.step(dve.tensor_copy(pad[:, 0:TILES, 0:GROUPS],
                                     bank[2][:, 0:TILES * ROUTES].rearrange("p (t n) -> p t n", t=TILES)[:, :, 0:GROUPS]))
            best(0)
            dve.tensor_scalar(gsm[:, 0, :], top[:, 0:TILES, 0], -1.0, None, ALU.mult).then_inc(gate_in, 1)
            own.step(dve.tensor_tensor(pick[:, :, :], iota16[:, 0:GROUPS].unsqueeze(1).to_broadcast([P, TILES, GROUPS]),
                                       idx_f[:, 0:TILES, 0:1].to_broadcast([P, TILES, GROUPS]), ALU.is_equal))
            for t in range(TILES):
                own.mark(dve.tensor_tensor(scr[:, t, :].rearrange("p (g e) -> p g e", g=GROUPS),
                                           logits[:, t, GROUPS:].rearrange("p (g e) -> p g e", g=GROUPS),
                                           pick[:, t, :].unsqueeze(2).to_broadcast([P, GROUPS, PER_GROUP]), ALU.mult))
            own.wait()
            own.step(dve.tensor_reduce(pad[:, TILES:2 * TILES, 0:PER_GROUP], scr[:, :, :].rearrange("p t (g e) -> p t e g", g=GROUPS),
                                       mybir.AxisListType.X, ALU.add))
            best(TILES)
            dve.wait_ge(gate_out, TILES)
            own.step(dve.reciprocal(gsm[:, 3, :], gsm[:, 1, :]))
            dve.tensor_tensor(gsm[:, 0, :], top[:, TILES:2 * TILES, 1], top[:, TILES:2 * TILES, 0], ALU.subtract).then_inc(gate_in, 1)
            for k in range(TOPK):
                own.mark(dve.scalar_tensor_tensor(out=eid[:, k, :], in0=idx_f[:, 0:TILES, 0], scalar=float(PER_GROUP),
                                                  in1=idx_f[:, TILES:2 * TILES, k], op0=ALU.mult, op1=ALU.add))
            own.wait()
            for k in range(TOPK):
                own.mark(dve.tensor_tensor(chosen[:, k, :, :], iota16[:, :].unsqueeze(1).to_broadcast([P, TILES, EXPERTS]),
                                           eid[:, k, :].unsqueeze(2).to_broadcast([P, TILES, EXPERTS]), ALU.is_equal))
            own.wait()
            dve.tensor_tensor(member[:, :, :], chosen[:, 0, :, :], chosen[:, 1, :, :], ALU.add).then_inc(member_ready, 1)
            dve.wait_ge(gate_out, TILES + 1)
            own.step(dve.tensor_scalar(gsm[:, 1, :], gsm[:, 2, :], 1.0, None, ALU.add))
            own.step(dve.reciprocal(gsm[:, 1, :], gsm[:, 1, :]))
            own.step(dve.tensor_tensor(weight[:, 0, :], gsm[:, 1, :], gsm[:, 3, :], ALU.mult))
            own.step(dve.tensor_tensor(weight[:, 1, :], weight[:, 0, :], gsm[:, 2, :], ALU.mult))
            dve.wait_ge(ranked, 1)
            for k in range(TOPK):
                own.step(dve.tensor_tensor(scr[:, :, :], bank[3][:, 0:TILES * EXPERTS].rearrange("p (t e) -> p t e", t=TILES),
                                           chosen[:, k, :, :], ALU.mult))
                own.step(dve.tensor_reduce(rank[:, k, :], scr[:, :, :], mybir.AxisListType.X, ALU.add))
            own.step(dve.tensor_scalar(turn_f[:, :, :], rank[:, :, :], float(P), None, ALU.is_ge))
            for c in range(2, SLOT_TURNS):
                own.step(dve.scalar_tensor_tensor(out=turn_f[:, :, :], in0=rank[:, :, :], scalar=float(c * P), in1=turn_f[:, :, :],
                                                  op0=ALU.is_ge, op1=ALU.add))
            own.step(dve.scalar_tensor_tensor(out=tmp_f[:, :, :], in0=rank[:, :, :], scalar=float(SLOT_TURNS * EXPERTS), in1=eid[:, :, :],
                                              op0=ALU.mult, op1=ALU.add))
            dve.scalar_tensor_tensor(out=row_i[:, :, :], in0=turn_f[:, :, :], scalar=float(EXPERTS - P * SLOT_TURNS * EXPERTS),
                                     in1=tmp_f[:, :, :], op0=ALU.mult, op1=ALU.add).then_inc(rows_known, 1)
            dve.wait_ge(counted, 1)
            own.step(dve.tensor_reduce(fullest[:, 0:1], bank[4][0:1, 0:EXPERTS], mybir.AxisListType.X, ALU.max))
            own.step(dve.tensor_scalar(turns_i[:, :], fullest[:, 0:1], float(P - 1), None, ALU.add))
            dve.tensor_scalar(turns_i[:, :], turns_i[:, :], 7, 2, ALU.logical_shift_right, ALU.logical_shift_left).then_inc(turns_ready, 1)
            dve.wait_ge(table_in, 16)
            dve.tensor_scalar(slot_of[:, :], slot_to[:, :], 1, None, ALU.logical_shift_right).then_inc(slots_ready, 1)

            dve.wait_ge(turns_ready, 1)
            turns = dve.value_load(turns_i[0:1, 0:1], min_val=EXPERT_TURNS, max_val=EXPERT_TURNS * SLOT_TURNS)
            dve.sem_inc(y1_copied, 1)
            with dve.Fori(0, turns) as it:
                own.enter(it, 3 * SETS)

                def swiglu(b):
                    gu = bank[2 + b % 2]
                    dve.wait_ge(sig_ready, it * SETS + b + 1)
                    own.step(dve.tensor_scalar(act_t[:, 1, :], act_t[:, 0, :], 1.0, None, ALU.add))
                    own.step(dve.reciprocal(act_t[:, 1, :], act_t[:, 1, :]))
                    own.step(dve.tensor_tensor(act_t[:, 2, :], gu[:, 0:DE], act_t[:, 1, :], ALU.mult))
                    dve.tensor_tensor(act_t[:, 3, :], gu[:, DE:2 * DE], act_t[:, 2, :], ALU.mult).then_inc(act_ready, 1)

                def evac_y1(b):
                    dve.wait_ge(y_done, it * (2 * SETS) + 2 * b + 2)
                    dve.wait_ge(scattered[b % 2], it * (16 * SETS // 2) + 16 * (b // 2 + 1))
                    dve.tensor_copy(y_slot[:, b % 2, 512:1024], bank[6][:, :]).then_inc(y1_copied, 1)

                for b in range(SETS):
                    swiglu(b)
                    if b:
                        evac_y1(b - 1)
                evac_y1(SETS - 1)

            for t in range(TILES):
                dve.wait_ge(y_in[t], 16)
                for k in range(TOPK):
                    ins = dve.scalar_tensor_tensor(out=x_rows[:, t, :], in0=y_pairs[t][:, k * D:(k + 1) * D],
                                                   scalar=weight[:, k, t:t + 1], in1=x_rows[:, t, :], op0=ALU.mult, op1=ALU.add)
                    ins.then_inc(x2_ready, 1)
                    dve.wait_ge(x2_ready, TOPK * t + k + 1)
            for t in range(TILES):
                dve.wait_ge(sq2_done, t + 1)
                variance(var[:, t:t + 1], ss[:, t:t + 1], D)
            end = Tally(dve, end_own)
            own = end
            dve.wait_ge(gain_in, 48)
            for t in range(TILES):
                dve.wait_ge(root_in, 9 + t)
                refine(var[:, t:t + 1], rs[:, t:t + 1], nt[:, t:t + 1])
                dve.scalar_tensor_tensor(out=h2_rows[:, t, :], in0=x_rows[:, t, :], scalar=rs[:, t:t + 1], in1=gain_row[:, :],
                                         op0=ALU.mult, op1=ALU.mult).then_inc(out_ready, 1)


def kernel(x, ln1_g, w_in, mix_norm_g, w_out, ln2_g, w_group_router, b_group_router, w_expert_router,
           b_expert_router, w_gate, w_up, w_down, final_norm_g):
    import numpy as np
    import concourse.bacc as bacc
    from concourse.bass_utils import run_bass_kernel_spmd

    heads = [*range(0, 4), *range(8, 16), *range(4, 8)]
    cont = np.ascontiguousarray
    wi = np.asarray(w_in)[0].reshape(KC, P, 3, HEADS, HD)[:, :, :, heads].reshape(KC, P, 3, PAIRS, P)
    gate, up = (np.asarray(w)[0].reshape(EXPERTS, KC, P, DE) for w in (w_gate, w_up))
    gu = np.concatenate([gate, up], axis=-1).transpose(0, 2, 1, 3).reshape(EXPERTS, P, KC * 2 * DE)
    down = np.asarray(w_down)[0].reshape(EXPERTS, RC, P, D).transpose(0, 2, 1, 3).reshape(EXPERTS, P, RC * D)
    route = np.concatenate([np.asarray(w_group_router)[0],
                            np.asarray(w_expert_router)[0].transpose(1, 0, 2).reshape(D, EXPERTS)], axis=-1)
    arrays = {
        "x": cont(np.asarray(x)[0]),
        "gain1": cont(np.asarray(ln1_g)[0]),
        "w_qkv": cont(wi.transpose(3, 1, 2, 0, 4).reshape(PAIRS, P, 3 * KC * P)),
        "gain_mix": cont(np.asarray(mix_norm_g)[0].reshape(HEADS, HD)[heads].reshape(PAIRS, P).T),
        "w_out": cont(np.asarray(w_out)[0].reshape(HEADS, HD, D)[heads].reshape(PAIRS, P, D).transpose(1, 0, 2).reshape(P, PAIRS * D)),
        "gain2": cont(np.asarray(ln2_g)[0]),
        "w_route": cont(route.reshape(KC, P, ROUTES).transpose(1, 0, 2).reshape(P, KC * ROUTES)),
        "b_route": cont(np.concatenate([np.asarray(b_group_router)[0], np.asarray(b_expert_router)[0].reshape(EXPERTS)])[None]),
        "w_expert": cont(np.concatenate([gu, down], axis=-1)),
        "gain_final": cont(np.asarray(final_norm_g)),
    }
    nc = bacc.Bacc("TRN2", target_bir_lowering=False, num_devices=1)
    args = [nc.dram_tensor(n, a.shape, mybir.dt.float32, kind="ExternalInput").ap() for n, a in arrays.items()]
    out = nc.dram_tensor("out", (SEQ, D), mybir.dt.float32, kind="ExternalOutput").ap()
    decoder_layer(nc, *args, out)
    r = run_bass_kernel_spmd(nc, [arrays], core_ids=[0])
    return r.results[0]["out"].reshape(1, SEQ, D)
```

```python
import concourse.bass as bass
from concourse import mybir
from contextlib import ExitStack

P = 128
SEQ, D = 512, 1024
HEADS, HD = 16, 64
TILES = SEQ // P
KC = D // P
PAIRS = HEADS // 2
SOFT_PAIRS = 6
GROUPS, PER_GROUP = 4, 4
EXPERTS = GROUPS * PER_GROUP
DE = D // 4
RC = DE // P
ROUTES = GROUPS + EXPERTS
TOPK = 2
SLOT_TURNS = SEQ // P
EPS = 1e-6
NEG = -1e30
UNITS = 2 * TILES
SETS = 4
EXPERT_TURNS = EXPERTS // SETS
WORDS = KC * 2 * DE + RC * D
COLS = SLOT_TURNS * EXPERTS
BIG = 1 << 20
SLOPES = [2.0 ** (-8.0 * (i + 1) / 4) for i in range(4)] + [2.0 ** (-8.0 * (i + 1) / 8) for i in range(8)]
MIX_GROUPS = [(0, 2), (2, 6), (6, 8)]


class Tally:

    def __init__(self, eng, sem):
        self.eng, self.sem, self.n, self.offset = eng, sem, 0, None

    def now(self):
        return self.n if self.offset is None else self.offset + self.n

    def mark(self, ins):
        ins.then_inc(self.sem, 1)
        self.n += 1
        return self.now()

    def wait(self, value=None):
        self.eng.wait_ge(self.sem, self.now() if value is None else value)

    def step(self, ins):
        self.mark(ins)
        self.wait()

    def enter(self, turn, per):
        self.first, self.per, self.offset = self.n, per, turn * per

    def leave(self, turns):
        assert self.n - self.first == self.per, (self.n - self.first, self.per)
        self.n, self.offset = self.first + turns * self.per, None


def decoder_layer(nc, x, gain1, w_qkv, gain_mix, w_out, gain2, w_route, b_route, w_expert, gain_final, out):
    F32, I32 = mybir.dt.float32, mybir.dt.int32
    U32 = mybir.dt.uint32
    ALU, ACT = mybir.AluOpType, mybir.ActivationFunctionType

    ctx = ExitStack()
    with ctx:
        def sb(name, shape, dt=F32):
            return ctx.enter_context(nc.sbuf_tensor(name, shape, dt))

        def sem(name):
            return ctx.enter_context(nc.semaphore(name))

        x_rows = sb("x_rows", [P, TILES, D])
        gain_row = sb("gain_row", [P, D])
        set0 = sb("set0", [P, WORDS])
        mixer_w = sb("mixer_w", [P, PAIRS * D])
        wo = mixer_w[:, :].rearrange("p (c n) -> p c n", c=PAIRS)
        attn = sb("attn", [P, WORDS])
        o_all = sb("o_all", [P, PAIRS, SEQ])
        wide = sb("wide", [P, 2 * TILES * SEQ])

        at = [0]

        def part(region, words):
            at[0] += words
            return region[:, at[0] - words:at[0]]

        prob = part(attn, 4 * SEQ).rearrange("p (r n) -> p r n", r=4)
        qT, kT = part(attn, SEQ), part(attn, SEQ)
        v_tok = part(attn, SEQ).rearrange("p (j d) -> p j d", j=TILES)
        bias = part(attn, 2 * SEQ).rearrange("p (a n) -> p a n", a=2)
        log_count = part(attn, 2 * SEQ).rearrange("p (a n) -> p a n", a=2)
        neg_dist = part(attn, SEQ)
        assert at[0] <= WORDS
        probT = wide[:, :].rearrange("p (a j q) -> p a j q", a=2, j=TILES)
        SB_W = [SEQ - P * j for j in range(TILES)]
        SB_AT = [sum(SB_W[:j]) for j in range(TILES)]
        sb_n = sum(SB_W)
        vT = sb("vT", [P, SEQ])
        soft = [wide[:, a * sb_n:(a + 1) * sb_n] for a in range(2)]
        stick = [wide[:, 2 * sb_n:3 * sb_n], attn[:, 0:sb_n]]
        h_rows = o_all[:, :, :].rearrange("p c t -> p (c t)").rearrange("p (t d) -> p t d", t=TILES)
        h2_rows = wide[:, :].rearrange("p (t d) -> p t d", t=TILES)
        ident, ones = sb("ident", [P, P]), sb("ones", [P, P])
        neg_tri, neg_ones, before = sb("neg_tri", [P, P]), sb("neg_ones", [P, P]), sb("before", [P, P])
        slope = sb("slope", [P, 2 * SOFT_PAIRS])
        dist_i = wide[:, 0:SEQ].bitcast(I32)
        mod_i = wide[:, SEQ:2 * SEQ].bitcast(I32)
        hits, count = wide[:, 2 * SEQ:3 * SEQ], wide[:, 3 * SEQ:4 * SEQ]
        gain_m = sb("gain_m", [P, PAIRS])
        wr = sb("wr", [P, KC, ROUTES])
        br = sb("br", [1, ROUTES])
        ss = sb("ss", [P, TILES])
        var, rs, nt = sb("var", [P, TILES]), sb("rs", [P, TILES]), sb("nt", [P, TILES])
        neg_max, den, rden = sb("neg_max", [P, UNITS]), sb("den", [P, UNITS]), sb("rden", [P, UNITS])
        logits = sb("logits", [P, TILES, ROUTES])
        pad = sb("pad", [P, 2 * TILES, 8])
        top = sb("top", [P, 2 * TILES, 8])
        top_i = sb("top_i", [P, 2 * TILES, 8], U32)
        idx_f = sb("idx_f", [P, 2 * TILES, 2])
        iota = sb("iota", [P, P])
        pick = sb("pick", [P, TILES, GROUPS])
        scr = sb("scr", [P, TILES, EXPERTS])
        chosen = sb("chosen", [P, TOPK, TILES, EXPERTS])
        member = sb("member", [P, TILES, EXPERTS])
        eid = sb("eid", [P, TOPK, TILES])
        rank = sb("rank", [P, TOPK, TILES])
        turn_f = sb("turn_f", [P, TOPK, TILES])
        tmp_f = sb("tmp_f", [P, TOPK, TILES])
        slot_f = sb("slot_f", [P, TOPK, TILES])
        token_f = sb("token_f", [P, TOPK, TILES])
        weight = sb("weight", [P, TOPK, TILES])
        gsm = sb("gsm", [P, 4, TILES])
        group_exp = sb("group_exp", [P, TILES, GROUPS])
        taken = sb("taken", [P, COLS])
        slot_to = sb("slot_to", [P, COLS + SETS], I32)
        slot_of = sb("slot_of", [P, COLS + SETS], I32)
        gather_at, scatter_at = sb("gather_at", [P, SETS], I32), sb("scatter_at", [P, SETS], I32)
        dve_tick, pool_tick = sb("dve_tick", [1, UNITS]), sb("pool_tick", [1, 2 * SETS])
        fullest = sb("fullest", [1, 4])
        turns_i = sb("turns_i", [1, 2], I32)

        with ExitStack() as projecting:
            def split(name, shape):
                return [projecting.enter_context(nc.sbuf_tensor(f"{name}_{part}", shape, mybir.dt.float32r))
                        for part in ("high", "low")]

            hT = split("hT", [P, KC, SEQ])
            w_even, w_odd = split("w_even", [P, KC, P]), split("w_odd", [P, KC, P])
            w_raw = projecting.enter_context(nc.sbuf_tensor("w_raw", [P, 2, KC, P], F32))
        w_split = [w_even, w_odd, w_even]
        w_whole = [w_raw[:, 0, :, :], w_raw[:, 1, :, :], w_raw[:, 0, :, :]]
        front = sb("front", [P, KC * SEQ + 3 * KC * P])
        set1 = sb("set1", [P, WORDS])
        sets = [set0[:, :], set1[:, :], mixer_w[:, 0:WORDS], attn[:, :]]
        h2T = front[:, 0:2 * D].rearrange("p (r c s) -> p r c s", r=2, c=KC)
        at[0] = 0
        x_slot = part(front, SETS * D).rearrange("p (r d) -> p r d", r=SETS)
        xT = part(front, 2 * D).rearrange("p (r c s) -> p r c s", r=2, c=KC)
        actT = part(front, 2 * DE).rearrange("p (r c s) -> p r c s", r=2, c=RC)
        assert at[0] <= KC * SEQ + 3 * KC * P
        y_slot = wide[:, :].rearrange("p (r d) -> p r d", r=SETS)
        o_flat = o_all[:, :, :].rearrange("p c t -> p (c t)")
        at[0] = 0
        act_t = part(o_flat, 4 * DE).rearrange("p (r f) -> p r f", r=4)
        slot_hot = part(o_flat, TOPK * TILES * P).rearrange("p (k t s) -> p k t s", k=TOPK, t=TILES)
        place_hot = part(o_flat, TOPK * TILES * COLS).rearrange("p (k t n) -> p k t n", k=TOPK, t=TILES)
        y_pairs = [set0[:, 0:2 * D], set0[:, 2 * D:4 * D], set1[:, 0:2 * D], set1[:, 2 * D:4 * D]]

        bank = [ctx.enter_context(nc.psum_tensor(f"bank{i}", [P, 512], F32)) for i in range(8)]
        S, T, O_BANK, PQ, PK, PV = bank[0:2], bank[2:4], bank[4], bank[5], bank[6], bank[7]

        h2_dram = nc.dram_tensor("h2_dram", [SEQ, D], F32).ap()
        y_dram = nc.dram_tensor("y_dram", [SEQ * TOPK, D], F32).ap()

        x_in, gain_in, small_in = [sem(f"x_in{t}") for t in range(TILES)], sem("gain_in"), sem("small_in")
        w_in = [sem(n) for n in ("wq_in", "wk_in", "wv_in")]
        w_high = [sem(n) for n in ("wq_high", "wk_high", "wv_high")]
        w_low = [sem(n) for n in ("wq_low", "wk_low", "wv_low")]
        wo_in, hT_high = sem("wo_in"), sem("hT_high")
        expert_in = [sem(f"expert_in{b}") for b in range(SETS)]
        pool_own, act_own, dve_own, end_own, act_end = (sem(n) for n in ("pool_own", "act_own", "dve_own", "end_own", "act_end"))
        consts_ready, squares_done, gain1_used = sem("consts_ready"), sem("squares_done"), sem("gain1_used")
        iota_ready, count_ready, log_ready = sem("iota_ready"), sem("count_ready"), sem("log_ready")
        rows_ready, turned, hT_ready = sem("rows_ready"), sem("turned"), sem("hT_ready")
        q_done, k_done, v_done = sem("q_done"), sem("k_done"), sem("v_done")
        qk_ready, vT_ready, v_turned, v_ready = sem("qk_ready"), sem("vT_ready"), sem("v_turned"), sem("v_ready")
        score_done, biased, exp_done, normed = sem("score_done"), sem("biased"), sem("exp_done"), sem("normed")
        prob_turned, probT_ready, pv_done, o_ready = sem("prob_turned"), sem("probT_ready"), sem("pv_done"), sem("o_ready")
        z_done, abs_done, ln_done, soft_ready = sem("z_done"), sem("abs_done"), sem("ln_done"), sem("soft_ready")
        stick_sum, stick_exp, stick_ready = sem("stick_sum"), sem("stick_exp"), sem("stick_ready")
        sq_ready, sq_summed, root_ready, y_ready = sem("sq_ready"), sem("sq_summed"), sem("root_ready"), sem("y_ready")
        root_in = sem("root_in")
        mixed, x1_ready, h2_ready, h2_stored = sem("mixed"), sem("x1_ready"), sem("h2_ready"), sem("h2_stored")
        turned2, h2T_ready, routed, logits_ready = sem("turned2"), sem("h2T_ready"), sem("routed"), sem("logits_ready")
        gate_in, gate_out = sem("gate_in"), sem("gate_out")
        member_ready, ranked, counted = sem("member_ready"), sem("ranked"), sem("counted")
        hot_ready, slots_done, slots_ready, turns_ready = sem("hot_ready"), sem("slots_done"), sem("slots_ready"), sem("turns_ready")
        gathered = [sem(f"gathered{b}") for b in range(SETS)]
        scattered = [sem(f"scattered{b}") for b in range(SETS)]
        xT_done, xT_ready, gu_done, sig_ready, act_ready = sem("xT_done"), sem("xT_ready"), sem("gu_done"), sem("sig_ready"), sem("act_ready")
        actT_done, actT_ready, y_done, y0_copied, y1_copied = sem("actT_done"), sem("actT_ready"), sem("y_done"), sem("y0_copied"), sem("y1_copied")
        y_in = [sem(f"y_in{t}") for t in range(TILES)]
        x2_ready, sq2_done, out_ready, stored = sem("x2_ready"), sem("sq2_done"), sem("out_ready"), sem("stored")

        block = ctx.enter_context(nc.Block())

        @block.sync
        def _(sp):
            for t in range(TILES):
                sp.dma_start(x_rows[:, t, :], x[t * P:(t + 1) * P, :]).then_inc(x_in[t], 16)
            sp.dma_start(gain_row[:, :], gain1.partition_broadcast(P)).then_inc(gain_in, 16)

            def load_w(n, w):
                sp.dma_start(w_whole[w], w_qkv[n, :, w * KC * P:(w + 1) * KC * P]
                             .rearrange("p (c m) -> p c m", c=KC)).then_inc(w_in[w], 16)

            load_w(0, 0)
            load_w(0, 1)
            sp.wait_ge(w_low[0], 1)
            load_w(0, 2)
            sp.dma_start(gain_m[:, :], gain_mix).then_inc(small_in, 16)
            sp.dma_start(wr[:, :, :], w_route.rearrange("p (c n) -> p c n", c=KC)).then_inc(small_in, 16)
            sp.dma_start(br[:, :], b_route).then_inc(small_in, 16)
            sp.dma_start(wo, w_out.rearrange("p (c n) -> p c n", c=PAIRS)).then_inc(wo_in, 16)
            sp.dma_start(sets[0], w_expert[0]).then_inc(expert_in[0], 16)
            sp.wait_ge(rows_ready, TILES)
            sp.dma_start(gain_row[:, :], gain2.partition_broadcast(P)).then_inc(gain_in, 16)
            with sp.Fori(1, PAIRS) as n:
                sp.wait_ge(w_low[2], n)
                load_w(n, 0)
                sp.wait_ge(w_low[1], n)
                load_w(n, 1)
                sp.wait_ge(w_low[0], n + 1)
                load_w(n, 2)
            sp.wait_ge(v_done, PAIRS)
            sp.dma_start(sets[1], w_expert[1]).then_inc(expert_in[1], 16)
            sp.wait_ge(mixed, TILES * 2)
            sp.dma_start(sets[2], w_expert[2]).then_inc(expert_in[2], 16)
            sp.dma_start(sets[3], w_expert[3]).then_inc(expert_in[3], 16)
            for t in range(TILES):
                sp.wait_ge(h2_ready, t + 1)
                sp.dma_start(h2_dram[t * P:(t + 1) * P, :], h2_rows[:, t, :]).then_inc(h2_stored, 16)
            sp.wait_ge(h2_ready, TILES)
            sp.dma_start(gain_row[:, :], gain_final.partition_broadcast(P)).then_inc(gain_in, 16)
            sp.wait_ge(turns_ready, 1)
            turns = sp.value_load(turns_i[0:1, 0:1], min_val=EXPERT_TURNS, max_val=EXPERT_TURNS * SLOT_TURNS)
            with sp.Fori(1, turns) as it:
                for b in range(SETS):
                    sp.wait_ge(y_done, it * (2 * SETS) + (2 * b + 2 - 2 * SETS))
                    sp.dma_start(sets[b], w_expert[(it % EXPERT_TURNS) * SETS + b, :, :]).then_inc(expert_in[b], 16)

            for b in range(SETS):
                sp.wait_ge(scattered[b], turns * 16)
            for t in range(TILES):
                sp.dma_start(y_pairs[t], y_dram[t * P * TOPK:(t + 1) * P * TOPK, :]
                             .rearrange("(p k) d -> p (k d)", k=TOPK)).then_inc(y_in[t], 16)
            for t in range(TILES):
                sp.wait_ge(out_ready, t + 1)
                sp.dma_start(out[t * P:(t + 1) * P, :], h2_rows[:, t, :]).then_inc(stored, 16)
            sp.wait_ge(stored, 16 * TILES)
            sp.wait_ge(h2_stored, 16 * TILES)

        @block.gpsimd
        def _(pool):
            own = Tally(pool, pool_own)
            pool.memset(ident[:, :], 0.0).then_inc(pool_own, 1)
            pool.memset(neg_tri[:, :], -1.0).then_inc(pool_own, 1)
            pool.memset(before[:, :], 1.0).then_inc(pool_own, 1)
            own.n = 3
            own.wait()
            own.mark(pool.affine_select(out=ident[:, :], in_=ident[:, :], compare_op=ALU.not_equal, fill=1.0,
                                        base=0, pattern=[[-1, P]], channel_multiplier=1))
            own.mark(pool.affine_select(out=neg_tri[:, :], in_=neg_tri[:, :], compare_op=ALU.is_ge, fill=0.0,
                                        base=0, pattern=[[-1, P]], channel_multiplier=1))
            own.mark(pool.affine_select(out=before[:, :], in_=before[:, :], compare_op=ALU.is_gt, fill=0.0,
                                        base=0, pattern=[[1, P]], channel_multiplier=-1))
            own.mark(pool.memset(ones[:, :], 1.0))
            own.mark(pool.memset(neg_ones[:, :], -1.0))
            own.wait()
            pool.memset(slot_to[:, COLS:], 2 * BIG).then_inc(consts_ready, 1)
            pool.iota(dist_i, pattern=[[-1, SEQ]], base=SEQ - P, channel_multiplier=1).then_inc(iota_ready, 1)
            pool.iota(neg_dist, pattern=[[1, SEQ]], base=P - SEQ, channel_multiplier=-1,
                      allow_small_or_imprecise_dtypes=True).then_inc(iota_ready, 1)
            pool.iota(iota[:, :], pattern=[[1, P]], base=0, channel_multiplier=0,
                      allow_small_or_imprecise_dtypes=True).then_inc(iota_ready, 1)
            pool.iota(token_f[:, :, :], pattern=[[1, TOPK], [TOPK * P, TILES]], base=1, channel_multiplier=TOPK,
                      allow_small_or_imprecise_dtypes=True).then_inc(iota_ready, 1)
            for h, s in enumerate(SLOPES):
                pool.memset(slope[:, h:h + 1], s).then_inc(iota_ready, 1)
            own.mark(pool.memset(log_count[:, 0, :], 0.0))
            own.wait()
            pool.wait_ge(log_ready, 1)
            for m in range(2):
                pool.affine_select(out=log_count[:, m, :], in_=log_count[:, m, :], compare_op=ALU.is_ge, fill=NEG,
                                   base=SEQ - P, pattern=[[-1, SEQ]], channel_multiplier=1).then_inc(log_ready, 1)
            pool.memset(pad[:, :, :], NEG).then_inc(consts_ready, 1)

            for g in range(2 * (PAIRS - SOFT_PAIRS)):
                for j in reversed(range(TILES)):
                    pool.wait_ge(stick_exp, g * TILES + TILES - j)
                    tile = stick[g % 2][:, SB_AT[j]:SB_AT[j] + P]
                    pool.affine_select(out=tile, in_=tile, compare_op=ALU.is_gt, fill=0.0,
                                       base=0, pattern=[[1, P]], channel_multiplier=-1).then_inc(stick_ready, 1)

            pool.wait_ge(h2_stored, 16 * TILES)
            pool.wait_ge(turns_ready, 1)
            pool.wait_ge(slots_ready, 1)
            turns = pool.value_load(turns_i[0:1, 0:1], min_val=EXPERT_TURNS, max_val=EXPERT_TURNS * SLOT_TURNS)
            last_token, last_row = pool.to_reg(SEQ - 1), pool.to_reg(SEQ * TOPK - 1)

            def gather(it, b):
                own.step(pool.tensor_copy(gather_at[:, b:b + 1], slot_of[:, bass.ds(it * SETS + b, 1)]))
                if not isinstance(it, int):
                    pool.tensor_tensor(pool_tick[:, b:b + 1], ones[0:1, 0:1], ones[0:1, 0:1], ALU.add)
                pool.indirect_dma_start(out=x_slot[:, b, :], out_offset=None, in_=h2_dram,
                                        in_offset=bass.IndirectOffsetOnAxis(ap=gather_at[:, b:b + 1].bitcast(U32), axis=0),
                                        bounds_check=last_token, oob_is_err=False).then_inc(gathered[b], 16)

            def scatter(it, b):
                pool.wait_ge(y0_copied, it * SETS + b + 1)
                pool.wait_ge(y1_copied, it * SETS + b + 1)
                own.step(pool.tensor_copy(scatter_at[:, b:b + 1], slot_to[:, bass.ds(it * SETS + b, 1)]))
                pool.tensor_tensor(pool_tick[:, SETS + b:SETS + b + 1], ones[0:1, 0:1], ones[0:1, 0:1], ALU.add)
                pool.indirect_dma_start(out=y_dram, out_offset=bass.IndirectOffsetOnAxis(ap=scatter_at[:, b:b + 1].bitcast(U32), axis=0),
                                        in_=y_slot[:, b, :], in_offset=None,
                                        bounds_check=last_row, oob_is_err=False).then_inc(scattered[b], 16)

            for b in range(SETS):
                gather(0, b)
            with pool.Fori(0, turns) as it:
                own.enter(it, 2 * SETS)
                for b in range(SETS):
                    pool.wait_ge(xT_done, it * SETS + b + 1)
                    gather(it + 1, b)
                    scatter(it, b)

        @block.tensor
        def _(pe):
            pe.wait_ge(consts_ready, 1)
            pe.wait_ge(rows_ready, TILES)
            for c in range(KC):
                if c >= 2:
                    pe.wait_ge(hT_ready, c - 1)
                for t in range(TILES):
                    mm = pe.transpose(S[c % 2][:, t * P:(t + 1) * P], h_rows[:, t, c * P:(c + 1) * P], ident[:, :])
                mm.then_inc(turned, 1)

            def project(n, w, dst, done):
                pe.wait_ge(w_low[w], n + 1)
                terms = ((0, 0), (1, 0), (0, 1))
                for c in range(KC):
                    for k, (of_w, of_h) in enumerate(terms):
                        mm = pe.matmul(dst[:, :], w_split[w][of_w][:, c, :], hT[of_h][:, c, :],
                                       start=(c + k == 0), stop=(c == KC - 1 and k == 2))
                mm.then_inc(done, 1)

            def turn_v(n):
                pe.wait_ge(vT_ready, n + 1)
                for j in range(TILES):
                    mm = pe.transpose(PV[:, j * P:(j + 1) * P], vT[:, j * P:(j + 1) * P], ident[:, :])
                mm.then_inc(v_turned, 1)

            pe.wait_ge(hT_ready, KC)
            project(0, 0, PQ, q_done)
            project(0, 1, PK, k_done)

            def scores(n, u):
                a, i = divmod(u, TILES)
                w = (i + 1) * P
                if u >= 2:
                    pe.wait_ge(biased, n * UNITS + (u - 1))
                h = slice(a * HD, (a + 1) * HD)
                pe.matmul(S[u % 2][:, 0:w], qT[h, i * P:w], kT[h, 0:w], start=True, stop=True).then_inc(score_done, 1)

            def turn(n, u):
                a, i = divmod(u, TILES)
                pe.wait_ge(normed, n * UNITS + (u + 1))
                if u >= 2:
                    pe.wait_ge(probT_ready, n * UNITS + (u - 1))
                for j in range(i + 1):
                    mm = pe.transpose(T[u % 2][:, j * P:(j + 1) * P], prob[:, u % 4, j * P:(j + 1) * P], ident[:, :])
                mm.then_inc(prob_turned, 1)

            def values(n, a, src, ready):
                ready()
                pe.wait_ge(v_ready, n + 1)
                if a == 0:
                    pe.wait_ge(o_ready, n + 1)
                for j in range(TILES):
                    mm = pe.matmul(O_BANK[a * HD:(a + 1) * HD, j * P:SEQ], v_tok[:, j, a * HD:(a + 1) * HD], src(j),
                                   start=(j == 0), stop=(j == TILES - 1), skip_group_check=True)
                mm.then_inc(pv_done, 1)

            with pe.Fori(0, SOFT_PAIRS) as n:
                pe.wait_ge(qk_ready, 2 * n + 2)
                for u in range(UNITS):
                    scores(n, u)
                    if u == 1:
                        project(n, 2, PV, v_done)
                    if u == 3:
                        turn_v(n)
                    if u >= 2:
                        turn(n, u - 2)
                    if u == 6:
                        values(n, 0, lambda j: probT[:, 0, j, j * P:SEQ],
                               lambda: pe.wait_ge(probT_ready, n * UNITS + TILES))
                project(n + 1, 0, PQ, q_done)
                turn(n, UNITS - 2)
                project(n + 1, 1, PK, k_done)
                turn(n, UNITS - 1)
                values(n, 1, lambda j: probT[:, 1, j, j * P:SEQ],
                       lambda: pe.wait_ge(probT_ready, n * UNITS + UNITS))

            Z = bank[0:4]

            def stick_z(n, a):
                g = 2 * (n - SOFT_PAIRS) + a
                h = slice(a * HD, (a + 1) * HD)
                for j in reversed(range(TILES)):
                    if g >= 1:
                        pe.wait_ge(stick_exp, (g - 1) * TILES + TILES - j)
                    pe.matmul(Z[j][:, 0:SB_W[j]], kT[h, j * P:(j + 1) * P], qT[h, j * P:SEQ], start=True, stop=False,
                              skip_group_check=True).then_inc(z_done, 1)

            def stick_tail(n, a):
                g = 2 * (n - SOFT_PAIRS) + a
                for j in reversed(range(TILES)):
                    pe.wait_ge(soft_ready, g * TILES + TILES - j)
                    for jj in reversed(range(j, TILES)):
                        mm = pe.matmul(Z[j][:, (jj - j) * P:SB_W[j]], (neg_tri if jj == j else neg_ones)[:, :],
                                       soft[a][:, SB_AT[jj]:SB_AT[jj] + SB_W[jj]], start=False, stop=(jj == j),
                                       skip_group_check=True)
                    mm.then_inc(stick_sum, 1)

            for n in range(SOFT_PAIRS, PAIRS):
                g = 2 * (n - SOFT_PAIRS)
                pe.wait_ge(qk_ready, 2 * n + 2)
                stick_z(n, 0)
                project(n, 2, PV, v_done)
                stick_tail(n, 0)
                turn_v(n)
                stick_z(n, 1)
                if n + 1 < PAIRS:
                    project(n + 1, 0, PQ, q_done)
                    project(n + 1, 1, PK, k_done)
                for a in range(2):
                    if a == 1:
                        stick_tail(n, 1)
                    values(n, a, lambda j, a=a: stick[a][:, SB_AT[j]:SB_AT[j] + SB_W[j]],
                           lambda a=a, g=g: pe.wait_ge(stick_ready, (g + a + 1) * TILES))

            for g, (lo, hi) in enumerate(MIX_GROUPS):
                for n in range(lo, hi):
                    pe.wait_ge(sq_ready, n + 1)
                    mm = pe.matmul(bank[g][:, :], ones[:, :], probT[:, n // TILES, n % TILES, :], start=(n == lo), stop=(n == hi - 1))
                mm.then_inc(sq_summed, 1)

            def turn_h2(t):
                pe.wait_ge(h2_ready, t + 1)
                for c in range(KC):
                    if c % 4 == 0 and t:
                        pe.wait_ge(h2T_ready, 2 * t - 1 + c // 4)
                    mm = pe.transpose(S[c // 4][:, (c % 4) * P:(c % 4 + 1) * P], h2_rows[:, t, c * P:(c + 1) * P], ident[:, :])
                    if c % 4 == 3:
                        mm.then_inc(turned2, 1)

            def route(t):
                o = bank[2][:, t * ROUTES:(t + 1) * ROUTES]
                pe.matmul(o, ones[0:1, :], br[:, :], start=True, stop=False)
                for c in range(KC):
                    if c % 4 == 0:
                        pe.wait_ge(h2T_ready, 2 * t + 1 + c // 4)
                    mm = pe.matmul(o, h2T[:, t % 2, c, :], wr[:, c, :], start=False, stop=(c == KC - 1))
                mm.then_inc(routed, 1)

            pe.wait_ge(wo_in, 16)
            pe.wait_ge(small_in, 48)
            pe.wait_ge(y_ready, PAIRS)
            for t in range(TILES):
                for half in range(2):
                    m = 2 * t + half
                    if m >= 2:
                        pe.wait_ge(x1_ready, m - 1)
                    for n in range(PAIRS):
                        mm = pe.matmul(bank[4 + m % 2][:, :], o_all[:, n, t * P:(t + 1) * P], wo[:, n, half * 512:(half + 1) * 512],
                                       start=(n == 0), stop=(n == PAIRS - 1))
                    mm.then_inc(mixed, 1)
                    if t and half == 0:
                        turn_h2(t - 1)
                if t:
                    route(t - 1)
            turn_h2(TILES - 1)
            route(TILES - 1)

            pe.wait_ge(member_ready, 1)
            for t in range(TILES):
                for s in range(t + 1):
                    mm = pe.matmul(bank[3][:, t * EXPERTS:(t + 1) * EXPERTS], (before if s == t else ones)[:, :], member[:, s, :],
                                   start=(s == 0), stop=(s == t))
            mm.then_inc(ranked, 1)
            for t in range(TILES):
                mm = pe.matmul(bank[4][0:1, 0:EXPERTS], ones[:, 0:1], member[:, t, :], start=(t == 0), stop=(t == TILES - 1))
            mm.then_inc(counted, 1)

            pe.wait_ge(hot_ready, 1)
            for k in range(TOPK):
                for t in range(TILES):
                    mm = pe.matmul(bank[5][:, 0:COLS], slot_hot[:, k, t, :], place_hot[:, k, t, :],
                                   start=(k == 0 and t == 0), stop=(k == TOPK - 1 and t == TILES - 1))
            mm.then_inc(slots_done, 1)

            XT, GU, AT, Y = bank[0:2], bank[2:4], bank[4], bank[5:7]

            def turn_rows(it, b):
                pe.wait_ge(gathered[b], it * 16 + 16)
                for c in range(KC):
                    if c % 4 == 0 and not (isinstance(it, int) and it + b == 0):
                        pe.wait_ge(xT_ready, it * (2 * SETS) + 2 * b - 1 + c // 4)
                    mm = pe.transpose(XT[c // 4][:, (c % 4) * P:(c % 4 + 1) * P], x_slot[:, b, c * P:(c + 1) * P], ident[:, :])
                mm.then_inc(xT_done, 1)

            def gate_up(it, b, half):
                w = sets[b][:, 0:KC * 2 * DE].rearrange("p (c f) -> p c f", c=KC)
                if half == 0:
                    pe.wait_ge(expert_in[b], it * 16 + 16)
                    if not (isinstance(it, int) and b < 2):
                        pe.wait_ge(act_ready, it * SETS + b - 1)
                pe.wait_ge(xT_ready, it * (2 * SETS) + 2 * b + half + 1)
                for c in range(half * 4, half * 4 + 4):
                    mm = pe.matmul(GU[b % 2][:, :], xT[:, b % 2, c, :], w[:, c, :], start=(c == 0), stop=(c == KC - 1))
                if half:
                    mm.then_inc(gu_done, 1)

            def turn_act(it, b):
                pe.wait_ge(act_ready, it * SETS + b + 1)
                for c in range(RC):
                    mm = pe.transpose(AT[:, c * P:(c + 1) * P], act_t[:, 3, c * P:(c + 1) * P], ident[:, :])
                mm.then_inc(actT_done, 1)

            def down(it, b):
                w = sets[b][:, KC * 2 * DE:].rearrange("p (c d) -> p c d", c=RC)
                pe.wait_ge(actT_ready, it * SETS + b + 1)
                for half in range(2):
                    if not (isinstance(it, int) and it * SETS + b == 0):
                        pe.wait_ge((y0_copied, y1_copied)[half], it * SETS + b)
                    for c in range(RC):
                        mm = pe.matmul(Y[half][:, :], actT[:, b % 2, c, :], w[:, c, half * 512:(half + 1) * 512],
                                       start=(c == 0), stop=(c == RC - 1))
                    mm.then_inc(y_done, 1)

            def expert_step(it, b, first=False):
                before = (it, b - 1) if b else (it - 1, SETS - 1)
                gate_up(it, b, 0)
                if not first:
                    turn_act(*before)
                gate_up(it, b, 1)
                turn_rows(*((it, b + 1) if b + 1 < SETS else (it + 1, 0)))
                if not first:
                    down(*before)

            pe.wait_ge(turns_ready, 1)
            turns = pe.value_load(turns_i[0:1, 0:1], min_val=EXPERT_TURNS, max_val=EXPERT_TURNS * SLOT_TURNS)
            last = pe.value_load(turns_i[0:1, 1:2], min_val=EXPERT_TURNS - 1, max_val=EXPERT_TURNS * SLOT_TURNS - 1)
            turn_rows(0, 0)
            for b in range(SETS):
                expert_step(0, b, first=(b == 0))
            with pe.Fori(1, turns) as it:
                for b in range(SETS):
                    expert_step(it, b)
            turn_act(last, SETS - 1)
            down(last, SETS - 1)

        @block.scalar
        def _(act):
            own = Tally(act, act_own)
            act.preload_act_table_set("natural_log_exp_and_others")

            def root(v, r, wait, done):
                wait()
                own.step(act.activation(r, v, ACT.Ln))
                act.activation(r, r, ACT.Exp, scale=-0.5).then_inc(done, 1)

            for t in range(TILES):
                act.wait_ge(x_in[t], 16)
                act.activation(h_rows[:, t, :], x_rows[:, t, :], ACT.Square, accum_out=ss[:, t:t + 1]).then_inc(squares_done, 1)
            root(var[:, :], rs[:, :], lambda: act.wait_ge(root_in, 1), root_ready)

            def split_high(n, w):
                act.wait_ge(w_in[w], n * 16 + 16)
                if w == 2:
                    act.wait_ge(q_done, n + 1)
                elif not isinstance(n, int) or n:
                    act.wait_ge((v_done, k_done)[w], n)
                act.activation(w_split[w][0][:, :, :], w_whole[w], ACT.Copy).then_inc(w_high[w], 1)

            split_high(0, 0)
            split_high(0, 1)
            for c in range(KC):
                act.wait_ge(turned, c + 1)
                act.activation(hT[0][:, c, :], S[c % 2][:, :], ACT.Copy).then_inc(hT_high, 1)
            act.wait_ge(count_ready, 1)
            act.activation(log_count[:, 1, :], count, ACT.Ln).then_inc(count_ready, 1)

            def evac_q(n):
                act.wait_ge(q_done, n + 1)
                act.activation(qT, PQ[:, :], ACT.Copy, scale=HD ** -0.5).then_inc(qk_ready, 1)

            def evac_k(n):
                act.wait_ge(k_done, n + 1)
                act.activation(kT, PK[:, :], ACT.Copy).then_inc(qk_ready, 1)

            evac_q(0)
            split_high(0, 2)
            evac_k(0)

            def exponent(n, u):
                a, i = divmod(u, TILES)
                w = (i + 1) * P
                act.wait_ge(biased, n * UNITS + (u + 1))
                act.activation(prob[:, u % 4, 0:w], prob[:, u % 4, 0:w], ACT.Exp, bias=neg_max[:, u:u + 1], scale=-1.0,
                               accum_out=den[:, u:u + 1]).then_inc(exp_done, 1)

            def store_T(n, u):
                a, i = divmod(u, TILES)
                act.wait_ge(prob_turned, n * UNITS + (u + 1))
                act.activation(probT[:, a, 0:i + 1, i * P:(i + 1) * P],
                               T[u % 2][:, 0:(i + 1) * P].rearrange("p (j q) -> p j q", q=P), ACT.Copy).then_inc(probT_ready, 1)

            with act.Fori(0, SOFT_PAIRS) as n:
                for u in range(UNITS):
                    exponent(n, u)
                    if u >= 2:
                        store_T(n, u - 2)
                    if u in (4, 5):
                        split_high(n + 1, u - 4)
                evac_q(n + 1)
                split_high(n + 1, 2)
                store_T(n, UNITS - 2)
                evac_k(n + 1)
                store_T(n, UNITS - 1)

            for n in range(SOFT_PAIRS, PAIRS):
                for a in range(2):
                    g = 2 * (n - SOFT_PAIRS) + a
                    for j in reversed(range(TILES)):
                        cols = stick[a][:, SB_AT[j]:SB_AT[j] + SB_W[j]]
                        act.wait_ge(z_done, g * TILES + TILES - j)
                        if g >= 2:
                            act.wait_ge(pv_done, 2 * SOFT_PAIRS + g - 1)
                        own.step(act.activation(cols, bank[j][:, 0:SB_W[j]], ACT.Abs))
                        own.step(act.activation(cols, cols, ACT.Exp, scale=-1.0))
                        act.activation(cols, cols, ACT.Ln, bias=1.0).then_inc(ln_done, 1)
                    for j in reversed(range(TILES)):
                        cols = stick[a][:, SB_AT[j]:SB_AT[j] + SB_W[j]]
                        act.wait_ge(stick_sum, g * TILES + TILES - j)
                        act.activation(cols, bank[j][:, 0:SB_W[j]], ACT.Exp).then_inc(stick_exp, 1)
                    if a == 0 and n + 1 < PAIRS:
                        split_high(n + 1, 0)
                        split_high(n + 1, 1)
                    if a == 1 and n + 1 < PAIRS:
                        evac_q(n + 1)
                        split_high(n + 1, 2)
                        evac_k(n + 1)

            for n in range(PAIRS):
                act.wait_ge(o_ready, n + 2)
                if n == 0:
                    act.wait_ge(pv_done, 2 * PAIRS)
                act.activation(probT[:, n // TILES, n % TILES, :], o_all[:, n, :], ACT.Square).then_inc(sq_ready, 1)
            for g in range(3):
                root((kT, qT, bias[:, 0, :])[g], prob[:, g, :],
                     lambda g=g: act.wait_ge(root_in, 2 + g), root_ready)

            def evac_h2T(t):
                for half in range(2):
                    act.wait_ge(turned2, 2 * t + half + 1)
                    act.activation(h2T[:, t % 2, 4 * half:4 * half + 4, :],
                                   bank[half][:, :].rearrange("p (c s) -> p c s", c=4), ACT.Copy).then_inc(h2T_ready, 1)

            for t in range(TILES):
                act.wait_ge(x1_ready, 2 * t + 2)
                act.activation(h2_rows[:, t, :], x_rows[:, t, :], ACT.Square, accum_out=ss[:, t:t + 1]).then_inc(squares_done, 1)
                root(var[:, t:t + 1], rs[:, t:t + 1], lambda: act.wait_ge(root_in, 5 + t), root_ready)
                if t:
                    evac_h2T(t - 1)
            evac_h2T(TILES - 1)

            act.wait_ge(gate_in, 1)
            for t in range(TILES):
                act.activation(group_exp[:, t, :], logits[:, t, 0:GROUPS], ACT.Exp, bias=gsm[:, 0, t:t + 1],
                               accum_out=gsm[:, 1, t:t + 1]).then_inc(gate_out, 1)
            act.wait_ge(gate_in, 2)
            act.activation(gsm[:, 2, :], gsm[:, 0, :], ACT.Exp).then_inc(gate_out, 1)

            act.wait_ge(turns_ready, 1)
            turns = act.value_load(turns_i[0:1, 0:1], min_val=EXPERT_TURNS, max_val=EXPERT_TURNS * SLOT_TURNS)
            last = act.value_load(turns_i[0:1, 1:2], min_val=EXPERT_TURNS - 1, max_val=EXPERT_TURNS * SLOT_TURNS - 1)

            def evac_xT(it, b):
                act.wait_ge(xT_done, it * SETS + b + 1)
                for half in range(2):
                    act.activation(xT[:, b % 2, 4 * half:4 * half + 4, :],
                                   bank[half][:, :].rearrange("p (c s) -> p c s", c=4), ACT.Copy).then_inc(xT_ready, 1)

            def silu_exp(it, b):
                act.wait_ge(gu_done, it * SETS + b + 1)
                if not (isinstance(it, int) and it * SETS + b == 0):
                    act.wait_ge(act_ready, it * SETS + b)
                act.activation(act_t[:, 0, :], bank[2 + b % 2][:, 0:DE], ACT.Exp, scale=-1.0).then_inc(sig_ready, 1)

            def evac_actT(it, b):
                act.wait_ge(actT_done, it * SETS + b + 1)
                act.activation(actT[:, b % 2, :, :], bank[4][:, 0:DE].rearrange("p (c s) -> p c s", c=RC),
                               ACT.Copy).then_inc(actT_ready, 1)

            def evac_y0(it, b):
                act.wait_ge(y_done, it * (2 * SETS) + 2 * b + 1)
                if not isinstance(it, int):
                    act.wait_ge(scattered[b], it * 16)
                act.activation(y_slot[:, b, 0:512], bank[5][:, :], ACT.Copy).then_inc(y0_copied, 1)

            def expert_step(it, b, first=False):
                before = (it, b - 1) if b else (it - 1, SETS - 1)
                if not first:
                    evac_actT(*before)
                silu_exp(it, b)
                evac_xT(*((it, b + 1) if b + 1 < SETS else (it + 1, 0)))
                if not first:
                    evac_y0(*before)

            evac_xT(0, 0)
            for b in range(SETS):
                expert_step(0, b, first=(b == 0))
            with act.Fori(1, turns) as it:
                for b in range(SETS):
                    expert_step(it, b)
            evac_actT(last, SETS - 1)
            evac_y0(last, SETS - 1)

            own = Tally(act, act_end)
            for t in range(TILES):
                act.wait_ge(x2_ready, TOPK * (t + 1))
                act.activation(h2_rows[:, t, :], x_rows[:, t, :], ACT.Square, accum_out=ss[:, t:t + 1]).then_inc(sq2_done, 1)
                root(var[:, t:t + 1], rs[:, t:t + 1], lambda: act.wait_ge(root_in, 9 + t), root_ready)

        @block.vector
        def _(dve):
            own = Tally(dve, dve_own)
            roots = [0]

            def variance(v, total, n):
                dve.tensor_scalar(v, total, 1.0 / n, EPS, ALU.mult, ALU.add).then_inc(root_in, 1)

            def refine(v, r, tmp):
                roots[0] += 1
                dve.wait_ge(root_ready, roots[0])
                own.step(dve.tensor_tensor(tmp, r, r, ALU.mult))
                own.step(dve.tensor_tensor(tmp, tmp, v, ALU.mult))
                own.step(dve.tensor_scalar(tmp, tmp, -0.5, 1.5, ALU.mult, ALU.add))
                own.step(dve.tensor_tensor(r, r, tmp, ALU.mult))

            dve.wait_ge(squares_done, TILES)
            variance(var[:, :], ss[:, :], D)
            dve.wait_ge(root_in, 1)
            refine(var[:, :], rs[:, :], nt[:, :])
            dve.wait_ge(gain_in, 16)
            for t in range(TILES):
                dve.scalar_tensor_tensor(out=h_rows[:, t, :], in0=x_rows[:, t, :], scalar=rs[:, t:t + 1], in1=gain_row[:, :],
                                         op0=ALU.mult, op1=ALU.mult).then_inc(rows_ready, 1)

            def split_low(n, w):
                high, low = w_split[w]
                dve.wait_ge(w_high[w], n + 1)
                dve.tensor_tensor(low[:, :, :], w_whole[w], high[:, :, :].bitcast(F32), ALU.subtract).then_inc(w_low[w], 1)

            split_low(0, 0)
            split_low(0, 1)
            for c in range(KC):
                dve.wait_ge(hT_high, c + 1)
                dve.tensor_tensor(hT[1][:, c, :], S[c % 2][:, :], hT[0][:, c, :].bitcast(F32), ALU.subtract).then_inc(hT_ready, 1)
            dve.wait_ge(iota_ready, 4 + len(SLOPES))
            own.step(dve.tensor_scalar(count, neg_dist, float(-P), None, ALU.is_ge))
            for dilation in (4, 16):
                own.step(dve.tensor_scalar(mod_i, dist_i, dilation - 1, None, ALU.bitwise_and))
                own.step(dve.scalar_tensor_tensor(out=count, in0=mod_i, scalar=0.0, in1=count, op0=ALU.is_equal, op1=ALU.add))
            own.step(dve.tensor_scalar(hits, count, 0.0, NEG, ALU.is_equal, ALU.mult))
            dve.tensor_scalar(count, count, 1.0, None, ALU.max).then_inc(count_ready, 1)
            dve.wait_ge(count_ready, 2)
            dve.tensor_tensor(log_count[:, 1, :], log_count[:, 1, :], hits, ALU.add).then_inc(log_ready, 1)
            split_low(0, 2)
            dve.wait_ge(log_ready, 3)
            dve.sem_inc(o_ready, 1)

            def evac_vT(n):
                dve.wait_ge(v_done, n + 1)
                dve.tensor_copy(vT[:, :], PV[:, :]).then_inc(vT_ready, 1)

            def evac_v(n):
                dve.wait_ge(v_turned, n + 1)
                dve.tensor_copy(v_tok[:, :, :], PV[:, :].rearrange("p (j d) -> p j d", j=TILES)).then_inc(v_ready, 1)

            def bias_scores(n, u):
                a, i = divmod(u, TILES)
                w = (i + 1) * P
                dve.wait_ge(score_done, n * UNITS + (u + 1))
                dve.memset(dve_tick[:, u:u + 1], 0.0)
                dve.tensor_tensor_reduce(out=prob[:, u % 4, 0:w], in0=S[u % 2][:, 0:w], in1=bias[:, a, SEQ - w:SEQ],
                                         scale=-1.0, scalar=3e38, op0=ALU.add, op1=ALU.min,
                                         accum_out=neg_max[:, u:u + 1]).then_inc(biased, 1)

            def normalise(n, u):
                a, i = divmod(u, TILES)
                w = (i + 1) * P
                dve.wait_ge(exp_done, n * UNITS + (u + 1))
                own.step(dve.reciprocal(rden[:, u:u + 1], den[:, u:u + 1]))
                dve.tensor_scalar(prob[:, u % 4, 0:w], prob[:, u % 4, 0:w], rden[:, u:u + 1], None, ALU.mult).then_inc(normed, 1)

            def evac_o(n):
                dve.wait_ge(pv_done, 2 * n + 2)
                if isinstance(n, int):
                    dst = o_all[:, n, :]
                else:
                    dst = o_all[:, bass.ds(n, 1), :].rearrange("p a t -> p (a t)")
                dve.tensor_copy(dst, O_BANK[:, :]).then_inc(o_ready, 1)

            with dve.Fori(0, SOFT_PAIRS) as n:
                own.enter(n, 2 + UNITS)
                for a in range(2):
                    own.mark(dve.scalar_tensor_tensor(
                        out=bias[:, a, :], in0=neg_dist, scalar=slope[:, bass.ds(2 * n + a, 1)],
                        in1=log_count[:, bass.ds((n + 2) // 4, 1), :].rearrange("p a t -> p (a t)"),
                        op0=ALU.mult, op1=ALU.add))
                own.wait()
                for u in range(UNITS):
                    bias_scores(n, u)
                    if u == 2:
                        evac_vT(n)
                    if u == 4:
                        evac_v(n)
                    if u >= 1:
                        normalise(n, u - 1)
                    if u in (5, 6):
                        split_low(n + 1, u - 5)
                normalise(n, UNITS - 1)
                split_low(n + 1, 2)
                evac_o(n)
            own.leave(SOFT_PAIRS)

            for n in range(SOFT_PAIRS, PAIRS):
                for a in range(2):
                    g = 2 * (n - SOFT_PAIRS) + a
                    for j in reversed(range(TILES)):
                        cols = slice(SB_AT[j], SB_AT[j] + SB_W[j])
                        dve.wait_ge(ln_done, g * TILES + TILES - j)
                        own.step(dve.scalar_tensor_tensor(out=soft[a][:, cols], in0=bank[j][:, 0:SB_W[j]], scalar=0.0,
                                                          in1=stick[a][:, cols], op0=ALU.max, op1=ALU.add))
                        diag = soft[a][:, SB_AT[j]:SB_AT[j] + P]
                        dve.tensor_tensor(diag, diag, before[:, :], ALU.mult).then_inc(soft_ready, 1)
                    if a == 0:
                        evac_vT(n)
                        evac_v(n)
                        if n + 1 < PAIRS:
                            split_low(n + 1, 0)
                            split_low(n + 1, 1)
                if n + 1 < PAIRS:
                    split_low(n + 1, 2)
                evac_o(n)

            dve.wait_ge(small_in, 48)
            for g, (lo, hi) in enumerate(MIX_GROUPS):
                v = (kT, qT, bias[:, 0, :])[g]
                dve.wait_ge(sq_summed, g + 1)
                variance(v, bank[g][:, :], (hi - lo) * P)
                dve.wait_ge(root_in, 2 + g)
                refine(v, prob[:, g, :], bias[:, 1, :])
                for n in range(lo, hi):
                    dve.scalar_tensor_tensor(out=o_all[:, n, :], in0=o_all[:, n, :], scalar=gain_m[:, n:n + 1],
                                             in1=prob[:, g, :], op0=ALU.mult, op1=ALU.mult).then_inc(y_ready, 1)

            for t in range(TILES):
                for half in range(2):
                    cols = x_rows[:, t, half * 512:(half + 1) * 512]
                    dve.wait_ge(mixed, 2 * t + half + 1)
                    dve.tensor_tensor(cols, bank[4 + half][:, :], cols, ALU.add).then_inc(x1_ready, 1)
                dve.wait_ge(squares_done, TILES + t + 1)
                variance(var[:, t:t + 1], ss[:, t:t + 1], D)
                dve.wait_ge(root_in, 5 + t)
                refine(var[:, t:t + 1], rs[:, t:t + 1], nt[:, t:t + 1])
                dve.wait_ge(gain_in, 32)
                dve.scalar_tensor_tensor(out=h2_rows[:, t, :], in0=x_rows[:, t, :], scalar=rs[:, t:t + 1], in1=gain_row[:, :],
                                         op0=ALU.mult, op1=ALU.mult).then_inc(h2_ready, 1)

            def best(lo):
                for t in range(lo, lo + TILES):
                    own.mark(dve.max(out=top[:, t, :], in_=pad[:, t, :]))
                own.wait()
                for t in range(lo, lo + TILES):
                    own.mark(dve.max_index(out=top_i[:, t, :], in_max=top[:, t, :], in_values=pad[:, t, :]))
                own.wait()
                own.step(dve.tensor_copy(idx_f[:, lo:lo + TILES, :], top_i[:, lo:lo + TILES, 0:2]))

            dve.wait_ge(routed, TILES)
            dve.wait_ge(consts_ready, 2)
            own.mark(dve.tensor_copy(logits[:, :, :], bank[2][:, 0:TILES * ROUTES].rearrange("p (t n) -> p t n", t=TILES)))
            own.step(dve.tensor_copy(pad[:, 0:TILES, 0:GROUPS],
                                     bank[2][:, 0:TILES * ROUTES].rearrange("p (t n) -> p t n", t=TILES)[:, :, 0:GROUPS]))
            best(0)
            dve.tensor_scalar(gsm[:, 0, :], top[:, 0:TILES, 0], -1.0, None, ALU.mult).then_inc(gate_in, 1)
            own.step(dve.tensor_tensor(pick[:, :, :], iota[:, 0:GROUPS].unsqueeze(1).to_broadcast([P, TILES, GROUPS]),
                                       idx_f[:, 0:TILES, 0:1].to_broadcast([P, TILES, GROUPS]), ALU.is_equal))
            for t in range(TILES):
                own.mark(dve.tensor_tensor(scr[:, t, :].rearrange("p (g e) -> p g e", g=GROUPS),
                                           logits[:, t, GROUPS:].rearrange("p (g e) -> p g e", g=GROUPS),
                                           pick[:, t, :].unsqueeze(2).to_broadcast([P, GROUPS, PER_GROUP]), ALU.mult))
            own.wait()
            own.step(dve.tensor_reduce(pad[:, TILES:2 * TILES, 0:PER_GROUP], scr[:, :, :].rearrange("p t (g e) -> p t e g", g=GROUPS),
                                       mybir.AxisListType.X, ALU.add))
            best(TILES)
            dve.wait_ge(gate_out, TILES)
            own.step(dve.reciprocal(gsm[:, 3, :], gsm[:, 1, :]))
            dve.tensor_tensor(gsm[:, 0, :], top[:, TILES:2 * TILES, 1], top[:, TILES:2 * TILES, 0], ALU.subtract).then_inc(gate_in, 1)
            for k in range(TOPK):
                own.mark(dve.scalar_tensor_tensor(out=eid[:, k, :], in0=idx_f[:, 0:TILES, 0], scalar=float(PER_GROUP),
                                                  in1=idx_f[:, TILES:2 * TILES, k], op0=ALU.mult, op1=ALU.add))
            own.wait()
            for k in range(TOPK):
                own.mark(dve.tensor_tensor(chosen[:, k, :, :], iota[:, 0:EXPERTS].unsqueeze(1).to_broadcast([P, TILES, EXPERTS]),
                                           eid[:, k, :].unsqueeze(2).to_broadcast([P, TILES, EXPERTS]), ALU.is_equal))
            own.wait()
            dve.tensor_tensor(member[:, :, :], chosen[:, 0, :, :], chosen[:, 1, :, :], ALU.add).then_inc(member_ready, 1)
            dve.wait_ge(gate_out, TILES + 1)
            own.step(dve.tensor_scalar(gsm[:, 1, :], gsm[:, 2, :], 1.0, None, ALU.add))
            own.step(dve.reciprocal(gsm[:, 1, :], gsm[:, 1, :]))
            own.step(dve.tensor_tensor(weight[:, 0, :], gsm[:, 1, :], gsm[:, 3, :], ALU.mult))
            own.step(dve.tensor_tensor(weight[:, 1, :], weight[:, 0, :], gsm[:, 2, :], ALU.mult))
            dve.wait_ge(ranked, 1)
            for k in range(TOPK):
                own.step(dve.tensor_tensor(scr[:, :, :], bank[3][:, 0:TILES * EXPERTS].rearrange("p (t e) -> p t e", t=TILES),
                                           chosen[:, k, :, :], ALU.mult))
                own.step(dve.tensor_reduce(rank[:, k, :], scr[:, :, :], mybir.AxisListType.X, ALU.add))
            own.step(dve.tensor_scalar(turn_f[:, :, :], rank[:, :, :], float(P), None, ALU.is_ge))
            for c in range(2, SLOT_TURNS):
                own.step(dve.scalar_tensor_tensor(out=turn_f[:, :, :], in0=rank[:, :, :], scalar=float(c * P), in1=turn_f[:, :, :],
                                                  op0=ALU.is_ge, op1=ALU.add))
            own.mark(dve.scalar_tensor_tensor(out=slot_f[:, :, :], in0=turn_f[:, :, :], scalar=-float(P), in1=rank[:, :, :],
                                              op0=ALU.mult, op1=ALU.add))
            own.step(dve.scalar_tensor_tensor(out=tmp_f[:, :, :], in0=turn_f[:, :, :], scalar=float(EXPERTS), in1=eid[:, :, :],
                                              op0=ALU.mult, op1=ALU.add))
            for k in range(TOPK):
                for t in range(TILES):
                    own.mark(dve.tensor_scalar(slot_hot[:, k, t, :], iota[:, :], slot_f[:, k, t:t + 1], None, ALU.is_equal))
                    ins = dve.tensor_scalar(place_hot[:, k, t, :], iota[:, 0:COLS], tmp_f[:, k, t:t + 1], token_f[:, k, t:t + 1],
                                            ALU.is_equal, ALU.mult)
                    own.mark(ins)
            own.wait()
            dve.sem_inc(hot_ready, 1)
            dve.wait_ge(counted, 1)
            own.step(dve.tensor_reduce(fullest[:, 0:1], bank[4][0:1, 0:EXPERTS], mybir.AxisListType.X, ALU.max))
            own.step(dve.tensor_scalar(turns_i[:, 0:1], fullest[:, 0:1], float(P - 1), None, ALU.add))
            own.step(dve.tensor_scalar(turns_i[:, 0:1], turns_i[:, 0:1], 7, 2, ALU.logical_shift_right, ALU.logical_shift_left))
            dve.tensor_scalar(turns_i[:, 1:2], turns_i[:, 0:1], 1, None, ALU.subtract).then_inc(turns_ready, 1)
            dve.wait_ge(slots_done, 1)
            own.step(dve.tensor_scalar(taken[:, :], bank[5][:, 0:COLS], 0.0, 2.0 * BIG, ALU.is_equal, ALU.mult))
            own.step(dve.scalar_tensor_tensor(out=slot_to[:, 0:COLS], in0=bank[5][:, 0:COLS], scalar=-1.0, in1=taken[:, :],
                                              op0=ALU.add, op1=ALU.add))
            dve.tensor_scalar(slot_of[:, :], slot_to[:, :], 1, None, ALU.logical_shift_right).then_inc(slots_ready, 1)

            dve.wait_ge(turns_ready, 1)
            turns = dve.value_load(turns_i[0:1, 0:1], min_val=EXPERT_TURNS, max_val=EXPERT_TURNS * SLOT_TURNS)
            last = dve.value_load(turns_i[0:1, 1:2], min_val=EXPERT_TURNS - 1, max_val=EXPERT_TURNS * SLOT_TURNS - 1)

            def swiglu(it, b):
                gu = bank[2 + b % 2]
                dve.wait_ge(sig_ready, it * SETS + b + 1)
                own.step(dve.tensor_scalar(act_t[:, 1, :], act_t[:, 0, :], 1.0, None, ALU.add))
                own.step(dve.reciprocal(act_t[:, 1, :], act_t[:, 1, :]))
                own.step(dve.tensor_tensor(act_t[:, 2, :], gu[:, 0:DE], act_t[:, 1, :], ALU.mult))
                dve.tensor_tensor(act_t[:, 3, :], gu[:, DE:2 * DE], act_t[:, 2, :], ALU.mult).then_inc(act_ready, 1)

            def evac_y1(it, b):
                dve.wait_ge(y_done, it * (2 * SETS) + 2 * b + 2)
                if not isinstance(it, int):
                    dve.wait_ge(scattered[b], it * 16)
                dve.tensor_copy(y_slot[:, b, 512:1024], bank[6][:, :]).then_inc(y1_copied, 1)

            def expert_step(it, b, first=False):
                swiglu(it, b)
                if not first:
                    evac_y1(*((it, b - 1) if b else (it - 1, SETS - 1)))

            for b in range(SETS):
                expert_step(0, b, first=(b == 0))
            with dve.Fori(1, turns) as it:
                own.enter(it - 1, 3 * SETS)
                for b in range(SETS):
                    expert_step(it, b)
            evac_y1(last, SETS - 1)

            for t in range(TILES):
                dve.wait_ge(y_in[t], 16)
                for k in range(TOPK):
                    ins = dve.scalar_tensor_tensor(out=x_rows[:, t, :], in0=y_pairs[t][:, k * D:(k + 1) * D],
                                                   scalar=weight[:, k, t:t + 1], in1=x_rows[:, t, :], op0=ALU.mult, op1=ALU.add)
                    ins.then_inc(x2_ready, 1)
                    dve.wait_ge(x2_ready, TOPK * t + k + 1)
            for t in range(TILES):
                dve.wait_ge(sq2_done, t + 1)
                variance(var[:, t:t + 1], ss[:, t:t + 1], D)
            end = Tally(dve, end_own)
            own = end
            dve.wait_ge(gain_in, 48)
            for t in range(TILES):
                dve.wait_ge(root_in, 9 + t)
                refine(var[:, t:t + 1], rs[:, t:t + 1], nt[:, t:t + 1])
                dve.scalar_tensor_tensor(out=h2_rows[:, t, :], in0=x_rows[:, t, :], scalar=rs[:, t:t + 1], in1=gain_row[:, :],
                                         op0=ALU.mult, op1=ALU.mult).then_inc(out_ready, 1)


def kernel(x, ln1_g, w_in, mix_norm_g, w_out, ln2_g, w_group_router, b_group_router, w_expert_router,
           b_expert_router, w_gate, w_up, w_down, final_norm_g):
    import numpy as np
    import concourse.bacc as bacc
    from concourse.bass_utils import run_bass_kernel_spmd

    heads = [*range(0, 4), *range(8, 16), *range(4, 8)]
    cont = np.ascontiguousarray
    wi = np.asarray(w_in)[0].reshape(KC, P, 3, HEADS, HD)[:, :, :, heads].reshape(KC, P, 3, PAIRS, P)
    gate, up = (np.asarray(w)[0].reshape(EXPERTS, KC, P, DE) for w in (w_gate, w_up))
    gu = np.concatenate([gate, up], axis=-1).transpose(0, 2, 1, 3).reshape(EXPERTS, P, KC * 2 * DE)
    down = np.asarray(w_down)[0].reshape(EXPERTS, RC, P, D).transpose(0, 2, 1, 3).reshape(EXPERTS, P, RC * D)
    route = np.concatenate([np.asarray(w_group_router)[0],
                            np.asarray(w_expert_router)[0].transpose(1, 0, 2).reshape(D, EXPERTS)], axis=-1)
    arrays = {
        "x": cont(np.asarray(x)[0]),
        "gain1": cont(np.asarray(ln1_g)[0]),
        "w_qkv": cont(wi.transpose(3, 1, 2, 0, 4).reshape(PAIRS, P, 3 * KC * P)),
        "gain_mix": cont(np.asarray(mix_norm_g)[0].reshape(HEADS, HD)[heads].reshape(PAIRS, P).T),
        "w_out": cont(np.asarray(w_out)[0].reshape(HEADS, HD, D)[heads].reshape(PAIRS, P, D).transpose(1, 0, 2).reshape(P, PAIRS * D)),
        "gain2": cont(np.asarray(ln2_g)[0]),
        "w_route": cont(route.reshape(KC, P, ROUTES).transpose(1, 0, 2).reshape(P, KC * ROUTES)),
        "b_route": cont(np.concatenate([np.asarray(b_group_router)[0], np.asarray(b_expert_router)[0].reshape(EXPERTS)])[None]),
        "w_expert": cont(np.concatenate([gu, down], axis=-1)),
        "gain_final": cont(np.asarray(final_norm_g)),
    }
    nc = bacc.Bacc("TRN2", target_bir_lowering=False, num_devices=1)
    args = [nc.dram_tensor(n, a.shape, mybir.dt.float32, kind="ExternalInput").ap() for n, a in arrays.items()]
    out = nc.dram_tensor("out", (SEQ, D), mybir.dt.float32, kind="ExternalOutput").ap()
    decoder_layer(nc, *args, out)
    r = run_bass_kernel_spmd(nc, [arrays], core_ids=[0])
    return r.results[0]["out"].reshape(1, SEQ, D)
```

```python
import concourse.bass as bass
from concourse import mybir
from contextlib import ExitStack

P = 128
SEQ, D = 512, 1024
HEADS, HD = 16, 64
TILES = SEQ // P
KC = D // P
PAIRS = HEADS // 2
SOFT_PAIRS = 6
GROUPS, PER_GROUP = 4, 4
EXPERTS = GROUPS * PER_GROUP
DE = D // 4
RC = DE // P
ROUTES = GROUPS + EXPERTS
TOPK = 2
SLOT_TURNS = SEQ // P
EPS = 1e-6
NEG = -1e30
UNITS = 2 * TILES
SETS = 4
EXPERT_TURNS = EXPERTS // SETS
WORDS = KC * 2 * DE + RC * D
GU_WORDS = KC * 2 * DE
COLS = SLOT_TURNS * EXPERTS
WHOLE = 2
GU_SPLITS = (KC - WHOLE) // 2
BIG = 1 << 20
SLOPES = [2.0 ** (-8.0 * (i + 1) / 4) for i in range(4)] + [2.0 ** (-8.0 * (i + 1) / 8) for i in range(8)]
MIX_GROUPS = [(0, 2), (2, 6), (6, 8)]
MIX_STEPS = [(g, t, half) for g in range(3) for t in range(TILES) for half in range(2)]
MIX_BANKS = [5 + m % 2 if m < 4 * TILES else 3 + m % 4 for m in range(6 * TILES)]
K_FILLS = {2: (0, 2), 3: (2, 4), 4: (4, 5), 8: (5, 8)}
Q_FILLS = {4: (0, 2), 5: (2, 4), 6: (4, 6), 7: (6, 8)}
FILLS = [0, 3, 8, 11, 12, 4 * TILES]


class Tally:

    def __init__(self, eng, sem):
        self.eng, self.sem, self.n, self.offset = eng, sem, 0, None

    def now(self):
        return self.n if self.offset is None else self.offset + self.n

    def mark(self, ins):
        ins.then_inc(self.sem, 1)
        self.n += 1
        return self.now()

    def wait(self, value=None):
        self.eng.wait_ge(self.sem, self.now() if value is None else value)

    def step(self, ins):
        self.mark(ins)
        self.wait()

    def enter(self, turn, per):
        self.first, self.per, self.offset = self.n, per, turn * per

    def leave(self, turns):
        assert self.n - self.first == self.per, (self.n - self.first, self.per)
        self.n, self.offset = self.first + turns * self.per, None


def decoder_layer(nc, x, gain1, w_qkv, gain_mix, w_out, gain2, w_route, b_route, w_expert, gain_final, out):
    F32, I32 = mybir.dt.float32, mybir.dt.int32
    U32, BF16 = mybir.dt.uint32, mybir.dt.bfloat16
    ALU, ACT = mybir.AluOpType, mybir.ActivationFunctionType

    ctx = ExitStack()
    with ctx:
        def sb(name, shape, dt=F32):
            return ctx.enter_context(nc.sbuf_tensor(name, shape, dt))

        def sem(name):
            return ctx.enter_context(nc.semaphore(name))

        x_rows = sb("x_rows", [P, TILES, D])
        gain_row = sb("gain_row", [P, D])
        set0 = sb("set0", [P, WORDS])
        attn = sb("attn", [P, WORDS])
        o_all = sb("o_all", [P, PAIRS, SEQ])
        wide = sb("wide", [P, 2 * TILES * SEQ])

        at = [0]

        def part(region, words):
            at[0] += words
            return region[:, at[0] - words:at[0]]

        prob = part(attn, 4 * SEQ).rearrange("p (r n) -> p r n", r=4)
        qT, kT = part(attn, SEQ), part(attn, SEQ)
        v_tok = part(attn, SEQ).rearrange("p (j d) -> p j d", j=TILES)
        bias = part(attn, 2 * SEQ).rearrange("p (a n) -> p a n", a=2)
        log_count = part(attn, 2 * SEQ).rearrange("p (a n) -> p a n", a=2)
        neg_dist = part(attn, SEQ)
        assert at[0] <= WORDS
        probT = wide[:, :].rearrange("p (a j q) -> p a j q", a=2, j=TILES)
        SB_W = [SEQ - P * j for j in range(TILES)]
        SB_AT = [sum(SB_W[:j]) for j in range(TILES)]
        sb_n = sum(SB_W)
        vT = sb("vT", [P, SEQ])
        squares = [bias[:, 0, :], bias[:, 1, :], log_count[:, 0, :], log_count[:, 1, :], neg_dist, attn[:, sb_n:sb_n + SEQ]]
        soft = [wide[:, a * sb_n:(a + 1) * sb_n] for a in range(2)]
        stick = [wide[:, 2 * sb_n:3 * sb_n], attn[:, 0:sb_n]]
        h_rows = o_all[:, :, :].rearrange("p c t -> p (c t)").rearrange("p (t d) -> p t d", t=TILES)
        h2_rows = wide[:, :].rearrange("p (t d) -> p t d", t=TILES)
        ident, ones = sb("ident", [P, P]), sb("ones", [P, P])
        ones_b, before_b = sb("ones_b", [P, P], BF16), sb("before_b", [P, P], BF16)
        neg_tri, neg_ones, before = sb("neg_tri", [P, P]), sb("neg_ones", [P, P]), sb("before", [P, P])
        slope = sb("slope", [P, 2 * SOFT_PAIRS])
        dist_i = wide[:, 0:SEQ].bitcast(I32)
        mod_i = wide[:, SEQ:2 * SEQ].bitcast(I32)
        hits, count = wide[:, 2 * SEQ:3 * SEQ], wide[:, 3 * SEQ:4 * SEQ]
        gain_m = sb("gain_m", [P, PAIRS])
        mix_var, mix_root, mix_tmp = (sb(n, [P, 3 * TILES]) for n in ("mix_var", "mix_root", "mix_tmp"))
        wr = sb("wr", [P, KC, ROUTES])
        br = sb("br", [1, ROUTES])
        ss = sb("ss", [P, TILES])
        var, rs, nt = sb("var", [P, TILES]), sb("rs", [P, TILES]), sb("nt", [P, TILES])
        neg_max, den, rden = sb("neg_max", [P, UNITS]), sb("den", [P, UNITS]), sb("rden", [P, UNITS])
        logits = sb("logits", [P, TILES, ROUTES])
        pad = sb("pad", [P, 2 * TILES, 8])
        top = sb("top", [P, 2 * TILES, 8])
        top_i = sb("top_i", [P, 2 * TILES, 8], U32)
        idx_f = sb("idx_f", [P, 2 * TILES, 2])
        iota = sb("iota", [P, P])
        pick = sb("pick", [P, TILES, GROUPS])
        scr = sb("scr", [P, TILES, EXPERTS])
        chosen = sb("chosen", [P, TOPK, TILES, EXPERTS])
        member = sb("member", [P, TILES, EXPERTS], BF16)
        eid = sb("eid", [P, TOPK, TILES])
        rank = sb("rank", [P, TOPK, TILES])
        turn_f = sb("turn_f", [P, TOPK, TILES])
        tmp_f = sb("tmp_f", [P, TOPK, TILES])
        slot_f = sb("slot_f", [P, TOPK, TILES])
        token_low = sb("token_low", [P, TOPK, TILES])
        token_high = sb("token_high", [P, TOPK, TILES])
        weight = sb("weight", [P, TOPK, TILES])
        gsm = sb("gsm", [P, 4, TILES])
        group_exp = sb("group_exp", [P, TILES, GROUPS])
        taken = sb("taken", [P, COLS])
        slot_to = sb("slot_to", [P, COLS + SETS], I32)
        slot_of = sb("slot_of", [P, COLS + SETS], I32)
        gather_at, scatter_at = sb("gather_at", [P, SETS], I32), sb("scatter_at", [P, SETS], I32)
        dve_tick, pool_tick = sb("dve_tick", [1, UNITS]), sb("pool_tick", [1, 2 * SETS])
        fullest = sb("fullest", [1, 4])
        turns_i = sb("turns_i", [1, 2], I32)

        with ExitStack() as projecting:
            mixer_w = projecting.enter_context(nc.sbuf_tensor("mixer_w", [P, PAIRS * D], F32))
            wo = mixer_w[:, :].rearrange("p (c n) -> p c n", c=PAIRS)

            def split(name, shape):
                return [projecting.enter_context(nc.sbuf_tensor(f"{name}_{part}", shape, mybir.dt.float32r))
                        for part in ("high", "low")]

            hT = split("hT", [P, KC, SEQ])
            w_qv, w_k = split("w_qv", [P, KC, P]), split("w_k", [P, KC, P])
            w_raw = projecting.enter_context(nc.sbuf_tensor("w_raw", [P, 2, KC, P], F32))
        w_split = [w_qv, w_k, w_qv]
        w_whole = [w_raw[:, 0, :, :], w_raw[:, 1, :, :], w_raw[:, 0, :, :]]
        set2 = sb("set2", [P, WORDS])
        F32R = mybir.dt.float32r
        gu_high, gu_low = sb("gu_high", [P, KC - WHOLE, 2 * DE], F32R), sb("gu_low", [P, KC - WHOLE, 2 * DE], F32R)
        xT_high, xT_low = sb("xT_high", [P, 2, KC - WHOLE, P], F32R), sb("xT_low", [P, 2, KC - WHOLE, P], F32R)
        front = sb("front", [P, 2 * D + 2 * DE])
        set1 = sb("set1", [P, WORDS])
        sets = [set0[:, :], set1[:, :], set2[:, :], attn[:, :]]
        h2T = front[:, 0:2 * D].rearrange("p (r c s) -> p r c s", r=2, c=KC)
        at[0] = 0
        x_slot3 = part(front, D)
        xT = part(front, 2 * WHOLE * P).rearrange("p (r c s) -> p r c s", r=2, c=WHOLE)
        actT = part(front, 2 * DE).rearrange("p (r c s) -> p r c s", r=2, c=RC)
        y_slot = wide[:, :].rearrange("p (r d) -> p r d", r=SETS)
        o_flat = o_all[:, :, :].rearrange("p c t -> p (c t)")
        at[0] = 0
        act_t = part(o_flat, 4 * DE).rearrange("p (r f) -> p r f", r=4)
        x_slot = [part(o_flat, D) for b in range(3)] + [x_slot3]
        at[0] = 0
        slot_hot = part(front, TOPK * TILES * P // 2).bitcast(BF16).rearrange("p (n s) -> p n s", n=TOPK * TILES)
        place_hot, place_low, place_high = (part(front, TOPK * TILES * COLS // 2).bitcast(BF16)
                                            .rearrange("p (n s) -> p n s", n=TOPK * TILES) for _ in range(3))
        y_pairs = [set0[:, 0:2 * D], set0[:, 2 * D:4 * D], set1[:, 0:2 * D], set1[:, 2 * D:4 * D]]

        bank = [ctx.enter_context(nc.psum_tensor(f"bank{i}", [P, 512], F32)) for i in range(8)]
        S, T, O_BANK, PQ, PK, PV = bank[0:2], bank[2:4], bank[4], bank[5], bank[6], bank[7]

        h2_dram = nc.dram_tensor("h2_dram", [SEQ, D], F32).ap()
        y_dram = nc.dram_tensor("y_dram", [SEQ * TOPK, D], F32).ap()

        x_in, gain_in, small_in = [sem(f"x_in{t}") for t in range(TILES)], sem("gain_in"), sem("small_in")
        w_in = [sem(n) for n in ("wq_in", "wk_in", "wv_in")]
        w_high = [sem(n) for n in ("wq_high", "wk_high", "wv_high")]
        w_low = [sem(n) for n in ("wq_low", "wk_low", "wv_low")]
        wo_in, hT_high = sem("wo_in"), sem("hT_high")
        gu_in, down_in = [sem(f"gu_in{b}") for b in range(SETS)], [sem(f"down_in{b}") for b in range(SETS)]
        pool_own, act_own, dve_own, end_own, act_end = (sem(n) for n in ("pool_own", "act_own", "dve_own", "end_own", "act_end"))
        consts_ready, squares_done = sem("consts_ready"), sem("squares_done")
        iota_ready, count_ready, log_ready = sem("iota_ready"), sem("count_ready"), sem("log_ready")
        rows_ready, turned, hT_ready = sem("rows_ready"), sem("turned"), sem("hT_ready")
        q_done, k_done, v_done = sem("q_done"), sem("k_done"), sem("v_done")
        qk_ready, vT_ready, v_turned, v_ready = sem("qk_ready"), sem("vT_ready"), sem("v_turned"), sem("v_ready")
        score_done, biased, exp_done, normed = sem("score_done"), sem("biased"), sem("exp_done"), sem("normed")
        prob_turned, probT_ready, pv_done, o_ready = sem("prob_turned"), sem("probT_ready"), sem("pv_done"), sem("o_ready")
        z_done, ln_done, soft_ready = sem("z_done"), sem("ln_done"), sem("soft_ready")
        stick_sum, stick_exp, stick_ready = sem("stick_sum"), sem("stick_exp"), sem("stick_ready")
        sq_ready, sq_summed, root_ready, wo_scaled = sem("sq_ready"), sem("sq_summed"), sem("root_ready"), sem("wo_scaled")
        root_in = sem("root_in")
        mixed, x1_ready, h2_ready, h2_stored = sem("mixed"), sem("x1_ready"), sem("h2_ready"), sem("h2_stored")
        turned2, h2T_ready, routed = sem("turned2"), sem("h2T_ready"), sem("routed")
        gate_in, gate_out = sem("gate_in"), sem("gate_out")
        member_ready, ranked, counted = sem("member_ready"), sem("ranked"), sem("counted")
        hot_ready, slots_done, slots_ready, turns_ready = sem("hot_ready"), sem("slots_done"), sem("slots_ready"), sem("turns_ready")
        gathered = [sem(f"gathered{b}") for b in range(SETS)]
        scattered = [sem(f"scattered{b}") for b in range(SETS)]
        xT_done, gu_done, sig_ready, act_ready = sem("xT_done"), sem("gu_done"), sem("sig_ready"), sem("act_ready")
        xT_ready, xT_split = [sem("xT0_ready"), sem("xT1_ready")], sem("xT_split")
        gu_split, gu_ready = sem("gu_split"), sem("gu_ready")
        actT_done, actT_ready, y_done, y0_copied, y1_copied = sem("actT_done"), sem("actT_ready"), sem("y_done"), sem("y0_copied"), sem("y1_copied")
        y_in = [sem(f"y_in{t}") for t in range(TILES)]
        x2_ready, sq2_done, stored = sem("x2_ready"), sem("sq2_done"), sem("stored")
        refined, scaled, out_ready = sem("refined"), sem("scaled"), [sem(f"out_ready{t}") for t in range(TILES)]

        def hT_part(part, t, half):
            return hT[part][:, 4 * half:4 * half + 4, t * P:(t + 1) * P], \
                bank[2 * (t % 2) + half][:, :].rearrange("p (c s) -> p c s", c=4)

        def gu_chunks(b, k):
            return sets[b][:, (WHOLE + 2 * k) * 2 * DE:(WHOLE + 2 * k + 2) * 2 * DE].rearrange("p (c f) -> p c f", c=2)

        def xT_chunks(lo, hi):
            return bank[lo // 4][:, lo % 4 * P:(lo % 4 + hi - lo) * P].rearrange("p (c s) -> p c s", c=hi - lo)

        block = ctx.enter_context(nc.Block())

        @block.sync
        def _(sp):
            for t in range(TILES):
                sp.dma_start(x_rows[:, t, :], x[t * P:(t + 1) * P, :]).then_inc(x_in[t], 16)
                if t == 0:
                    sp.dma_start(gain_row[:, :], gain1.partition_broadcast(P)).then_inc(gain_in, 16)

            def load_gu(e, b):
                sp.dma_start(sets[b][:, 0:GU_WORDS], w_expert[e, :, 0:GU_WORDS]).then_inc(gu_in[b], 16)

            def load_down(e, b):
                sp.dma_start(sets[b][:, GU_WORDS:], w_expert[e, :, GU_WORDS:]).then_inc(down_in[b], 16)

            def load_w(n, w):
                at = (1, 0, 2)[w]
                sp.dma_start(w_whole[w], w_qkv[n, :, at * KC * P:(at + 1) * KC * P]
                             .rearrange("p (c m) -> p c m", c=KC)).then_inc(w_in[w], 16)

            load_w(0, 0)
            load_w(0, 1)
            sp.wait_ge(w_low[0], 1)
            load_w(0, 2)
            sp.wait_ge(rows_ready, TILES)
            sp.dma_start(gain_row[:, :], gain2.partition_broadcast(P)).then_inc(gain_in, 16)
            sp.wait_ge(w_low[1], 1)
            load_w(1, 1)
            sp.wait_ge(w_low[2], 1)
            load_w(1, 0)
            sp.dma_start(gain_m[:, :], gain_mix).then_inc(small_in, 16)
            sp.dma_start(wr[:, :, :], w_route.rearrange("p (c n) -> p c n", c=KC)).then_inc(small_in, 16)
            sp.dma_start(br[:, :], b_route).then_inc(small_in, 16)
            sp.dma_start(wo, w_out.rearrange("p (c n) -> p c n", c=PAIRS)).then_inc(wo_in, 16)
            load_gu(0, 0)
            load_down(0, 0)
            sp.wait_ge(w_low[0], 2)
            load_w(1, 2)
            with sp.Fori(2, PAIRS) as n:
                sp.wait_ge(w_low[1], n)
                load_w(n, 1)
                sp.wait_ge(w_low[2], n)
                load_w(n, 0)
                sp.wait_ge(w_low[0], n + 1)
                load_w(n, 2)
            sp.wait_ge(v_done, PAIRS)
            load_gu(1, 1)
            load_down(1, 1)
            sp.wait_ge(sq_summed, PAIRS)
            load_gu(3, 3)
            load_down(3, 3)
            sp.wait_ge(mixed, len(MIX_STEPS))
            load_gu(2, 2)
            load_down(2, 2)
            for t in range(TILES):
                sp.wait_ge(h2_ready, t + 1)
                sp.dma_start(h2_dram[t * P:(t + 1) * P, :], h2_rows[:, t, :]).then_inc(h2_stored, 16)
            sp.wait_ge(h2_ready, TILES)
            sp.dma_start(gain_row[:, :], gain_final.partition_broadcast(P)).then_inc(gain_in, 16)
            sp.wait_ge(turns_ready, 1)
            turns = sp.value_load(turns_i[0:1, 0:1], min_val=EXPERT_TURNS, max_val=EXPERT_TURNS * SLOT_TURNS)
            with sp.Fori(1, turns) as it:
                for b in range(SETS + 1):
                    if b < SETS:
                        sp.wait_ge(gu_done, it * SETS + (b + 1 - SETS))
                        load_gu((it % EXPERT_TURNS) * SETS + b, b)
                    if b:
                        sp.wait_ge(y_done, it * (2 * SETS) + (2 * b - 2 * SETS))
                        load_down((it % EXPERT_TURNS) * SETS + (b - 1), b - 1)

            for b in range(SETS):
                sp.wait_ge(scattered[b], turns * 16)
            for t in range(TILES):
                sp.dma_start(y_pairs[t], y_dram[t * P * TOPK:(t + 1) * P * TOPK, :]
                             .rearrange("(p k) d -> p (k d)", k=TOPK)).then_inc(y_in[t], 16)
            for t in range(TILES):
                sp.wait_ge(out_ready[t], 1)
                sp.dma_start(out[t * P:(t + 1) * P, :], h2_rows[:, t, :]).then_inc(stored, 16)
            sp.wait_ge(stored, 16 * TILES)
            sp.wait_ge(h2_stored, 16 * TILES)

        @block.gpsimd
        def _(pool):
            own = Tally(pool, pool_own)
            pool.memset(ident[:, :], 0.0).then_inc(pool_own, 1)
            pool.memset(neg_tri[:, :], -1.0).then_inc(pool_own, 1)
            pool.memset(before[:, :], 1.0).then_inc(pool_own, 1)
            own.n = 3
            own.wait()
            own.mark(pool.affine_select(out=ident[:, :], in_=ident[:, :], compare_op=ALU.not_equal, fill=1.0,
                                        base=0, pattern=[[-1, P]], channel_multiplier=1))
            own.mark(pool.affine_select(out=neg_tri[:, :], in_=neg_tri[:, :], compare_op=ALU.is_ge, fill=0.0,
                                        base=0, pattern=[[-1, P]], channel_multiplier=1))
            own.mark(pool.affine_select(out=before[:, :], in_=before[:, :], compare_op=ALU.is_gt, fill=0.0,
                                        base=0, pattern=[[1, P]], channel_multiplier=-1))
            own.mark(pool.memset(ones[:, :], 1.0))
            own.mark(pool.memset(neg_ones[:, :], -1.0))
            own.wait()
            pool.memset(slot_to[:, COLS:], 2 * BIG).then_inc(consts_ready, 1)
            pool.iota(dist_i, pattern=[[-1, SEQ]], base=SEQ - P, channel_multiplier=1).then_inc(iota_ready, 1)
            pool.iota(neg_dist, pattern=[[1, SEQ]], base=P - SEQ, channel_multiplier=-1,
                      allow_small_or_imprecise_dtypes=True).then_inc(iota_ready, 1)
            pool.iota(iota[:, :], pattern=[[1, P]], base=0, channel_multiplier=0,
                      allow_small_or_imprecise_dtypes=True).then_inc(iota_ready, 1)
            pool.iota(token_low[:, :, :], pattern=[[1, TOPK], [0, TILES]], base=1, channel_multiplier=TOPK,
                      allow_small_or_imprecise_dtypes=True).then_inc(iota_ready, 1)
            pool.iota(token_high[:, :, :], pattern=[[0, TOPK], [TOPK * P, TILES]], base=0, channel_multiplier=0,
                      allow_small_or_imprecise_dtypes=True).then_inc(iota_ready, 1)
            for h, s in enumerate(SLOPES):
                pool.memset(slope[:, h:h + 1], s).then_inc(iota_ready, 1)
            own.mark(pool.memset(log_count[:, 0, :], 0.0))
            own.wait()
            pool.wait_ge(log_ready, 1)
            for m in range(2):
                pool.affine_select(out=log_count[:, m, :], in_=log_count[:, m, :], compare_op=ALU.is_ge, fill=NEG,
                                   base=SEQ - P, pattern=[[-1, SEQ]], channel_multiplier=1).then_inc(log_ready, 1)
            pool.tensor_copy(ones_b[:, :], ones[:, :]).then_inc(consts_ready, 1)
            pool.tensor_copy(before_b[:, :], before[:, :]).then_inc(consts_ready, 1)
            pool.memset(pad[:, :, :], NEG).then_inc(consts_ready, 1)

            for g in range(2 * (PAIRS - SOFT_PAIRS)):
                for j in reversed(range(TILES)):
                    pool.wait_ge(stick_exp, g * TILES + TILES - j)
                    tile = stick[g % 2][:, SB_AT[j]:SB_AT[j] + P]
                    pool.affine_select(out=tile, in_=tile, compare_op=ALU.is_gt, fill=0.0,
                                       base=0, pattern=[[1, P]], channel_multiplier=-1).then_inc(stick_ready, 1)

            pool.wait_ge(h2_stored, 16 * TILES)
            pool.wait_ge(turns_ready, 1)
            turns = pool.value_load(turns_i[0:1, 0:1], min_val=EXPERT_TURNS, max_val=EXPERT_TURNS * SLOT_TURNS)
            last_token, last_row = pool.to_reg(SEQ - 1), pool.to_reg(SEQ * TOPK - 1)
            pool.wait_ge(slots_ready, 1)

            def gather(it, b):
                if isinstance(it, int):
                    rows = slot_of[:, it * SETS + b:it * SETS + b + 1]
                else:
                    rows = gather_at[:, b:b + 1]
                    own.step(pool.tensor_copy(rows, slot_of[:, bass.ds(it * SETS + b, 1)]))
                    pool.tensor_tensor(pool_tick[:, b:b + 1], ones[0:1, 0:1], ones[0:1, 0:1], ALU.add)
                pool.indirect_dma_start(out=x_slot[b], out_offset=None, in_=h2_dram,
                                        in_offset=bass.IndirectOffsetOnAxis(ap=rows.bitcast(U32), axis=0),
                                        bounds_check=last_token, oob_is_err=False).then_inc(gathered[b], 16)

            def scatter(it, b):
                pool.wait_ge(y0_copied, it * SETS + b + 1)
                pool.wait_ge(y1_copied, it * SETS + b + 1)
                own.step(pool.tensor_copy(scatter_at[:, b:b + 1], slot_to[:, bass.ds(it * SETS + b, 1)]))
                pool.tensor_tensor(pool_tick[:, SETS + b:SETS + b + 1], ones[0:1, 0:1], ones[0:1, 0:1], ALU.add)
                pool.indirect_dma_start(out=y_dram, out_offset=bass.IndirectOffsetOnAxis(ap=scatter_at[:, b:b + 1].bitcast(U32), axis=0),
                                        in_=y_slot[:, b, :], in_offset=None,
                                        bounds_check=last_row, oob_is_err=False).then_inc(scattered[b], 16)

            for b in range(SETS):
                gather(0, b)
            with pool.Fori(0, turns) as it:
                own.enter(it, 2 * SETS)
                for b in range(SETS):
                    pool.wait_ge(xT_done, it * SETS + b + 1)
                    gather(it + 1, b)
                    scatter(it, b)

            pool.wait_ge(gain_in, 48)
            for t in range(2):
                pool.wait_ge(scaled, t + 1)
                pool.tensor_tensor(h2_rows[:, t, :], h2_rows[:, t, :], gain_row[:, :], ALU.mult).then_inc(out_ready[t], 1)

        @block.tensor
        def _(pe):
            pe.wait_ge(consts_ready, 1)
            for t in range(TILES):
                pe.wait_ge(rows_ready, t + 1)
                for half in range(2):
                    if t >= 2:
                        pe.wait_ge(hT_ready, 2 * (t - 2) + half + 1)
                    for c in range(4):
                        mm = pe.transpose(bank[2 * (t % 2) + half][:, c * P:(c + 1) * P],
                                          h_rows[:, t, (4 * half + c) * P:(4 * half + c + 1) * P], ident[:, :])
                    mm.then_inc(turned, 1)

            def project(n, w, dst, done, lo=0, hi=KC):
                if lo == 0:
                    pe.wait_ge(w_low[w], n + 1)
                terms = ((0, 0), (1, 0), (0, 1))
                for c in range(lo, hi):
                    for k, (of_w, of_h) in enumerate(terms):
                        mm = pe.matmul(dst[:, :], w_split[w][of_w][:, c, :], hT[of_h][:, c, :],
                                       start=(c + k == 0), stop=(c == KC - 1 and k == 2))
                if hi == KC:
                    mm.then_inc(done, 1)

            def turn_v(n):
                pe.wait_ge(vT_ready, n + 1)
                for j in range(TILES):
                    mm = pe.transpose(PV[:, j * P:(j + 1) * P], vT[:, j * P:(j + 1) * P], ident[:, :])
                mm.then_inc(v_turned, 1)

            pe.wait_ge(hT_ready, 2 * TILES)
            project(0, 0, PQ, q_done)
            project(0, 1, PK, k_done)

            def scores(n, u):
                a, i = divmod(u, TILES)
                w = (i + 1) * P
                if u >= 2:
                    pe.wait_ge(biased, n * UNITS + (u - 1))
                h = slice(a * HD, (a + 1) * HD)
                pe.matmul(S[u % 2][:, 0:w], qT[h, i * P:w], kT[h, 0:w], start=True, stop=True).then_inc(score_done, 1)

            def turn(n, u):
                a, i = divmod(u, TILES)
                pe.wait_ge(normed, n * UNITS + (u + 1))
                if u >= 2:
                    pe.wait_ge(probT_ready, n * UNITS + (u - 1))
                for j in range(i + 1):
                    mm = pe.transpose(T[u % 2][:, j * P:(j + 1) * P], prob[:, u % 4, j * P:(j + 1) * P], ident[:, :])
                mm.then_inc(prob_turned, 1)

            def values(n, a, src, ready):
                ready()
                pe.wait_ge(v_ready, n + 1)
                if a == 0:
                    pe.wait_ge(o_ready, n + 1)
                for j in range(TILES):
                    mm = pe.matmul(O_BANK[a * HD:(a + 1) * HD, j * P:SEQ], v_tok[:, j, a * HD:(a + 1) * HD], src(j),
                                   start=(j == 0), stop=(j == TILES - 1), skip_group_check=True)
                mm.then_inc(pv_done, 1)

            with pe.Fori(0, SOFT_PAIRS) as n:
                pe.wait_ge(qk_ready, 2 * n + 2)
                for u in range(UNITS):
                    scores(n, u)
                    if u == 1:
                        project(n, 2, PV, v_done)
                    if u == 3:
                        turn_v(n)
                    if u >= 2:
                        turn(n, u - 2)
                    if u in K_FILLS:
                        project(n + 1, 1, PK, k_done, *K_FILLS[u])
                    if u == 6:
                        values(n, 0, lambda j: probT[:, 0, j, j * P:SEQ],
                               lambda: pe.wait_ge(probT_ready, n * UNITS + TILES))
                    if u in Q_FILLS:
                        project(n + 1, 0, PQ, q_done, *Q_FILLS[u])
                turn(n, UNITS - 2)
                if UNITS in Q_FILLS:
                    project(n + 1, 0, PQ, q_done, *Q_FILLS[UNITS])
                if UNITS in K_FILLS:
                    project(n + 1, 1, PK, k_done, *K_FILLS[UNITS])
                turn(n, UNITS - 1)
                values(n, 1, lambda j: probT[:, 1, j, j * P:SEQ],
                       lambda: pe.wait_ge(probT_ready, n * UNITS + UNITS))

            Z = bank[0:4]

            def stick_z(n, a):
                g = 2 * (n - SOFT_PAIRS) + a
                h = slice(a * HD, (a + 1) * HD)
                for j in reversed(range(TILES)):
                    if g >= 1:
                        pe.wait_ge(stick_exp, (g - 1) * TILES + TILES - j)
                    pe.matmul(Z[j][:, 0:SB_W[j]], kT[h, j * P:(j + 1) * P], qT[h, j * P:SEQ], start=True, stop=False,
                              skip_group_check=True).then_inc(z_done, 1)

            def stick_tail(n, a):
                g = 2 * (n - SOFT_PAIRS) + a
                for j in reversed(range(TILES)):
                    pe.wait_ge(soft_ready, g * TILES + TILES - j)
                    for jj in reversed(range(j, TILES)):
                        mm = pe.matmul(Z[j][:, (jj - j) * P:SB_W[j]], (neg_tri if jj == j else neg_ones)[:, :],
                                       soft[a][:, SB_AT[jj]:SB_AT[jj] + SB_W[jj]], start=False, stop=(jj == j),
                                       skip_group_check=True)
                    mm.then_inc(stick_sum, 1)

            def sum_squares(lo, hi):
                for n in range(lo, hi):
                    g = [n < high for _, high in MIX_GROUPS].index(True)
                    pe.wait_ge(sq_ready, n + 1)
                    for t in range(TILES):
                        mm = pe.matmul(PV[:, g * TILES + t:g * TILES + t + 1], squares[n % len(squares)][:, t * P:(t + 1) * P], ones[:, 0:1],
                                       start=(n == lo and t == 0), stop=(n + 1 == hi), skip_group_check=True)
                    mm.then_inc(sq_summed, 1)

            def mix(first, end):
                for m in range(first, end):
                    g, t, half = MIX_STEPS[m]
                    bank_users = [i for i in range(m) if MIX_BANKS[i] == MIX_BANKS[m]]
                    if bank_users:
                        pe.wait_ge(x1_ready, bank_users[-1] + 1)
                    elif MIX_BANKS[m] == 4:
                        pe.wait_ge(o_ready, PAIRS + 1)
                    lo, hi = MIX_GROUPS[g]
                    if t + half == 0:
                        pe.wait_ge(wo_scaled, hi)
                        pe.wait_ge(o_ready, hi + 1)
                    for n in range(lo, hi):
                        mm = pe.matmul(bank[MIX_BANKS[m]][:, :], o_all[:, n, t * P:(t + 1) * P], wo[:, n, half * 512:(half + 1) * 512],
                                       start=(n == lo), stop=(n == hi - 1))
                    mm.then_inc(mixed, 1)

            def stick_values(n, a):
                values(n, a, lambda j: stick[a][:, SB_AT[j]:SB_AT[j] + SB_W[j]],
                       lambda: pe.wait_ge(stick_ready, (2 * (n - SOFT_PAIRS) + a + 1) * TILES))

            n = SOFT_PAIRS
            pe.wait_ge(qk_ready, 2 * n + 2)
            stick_z(n, 0)
            project(n, 2, PV, v_done)
            stick_tail(n, 0)
            turn_v(n)
            stick_z(n, 1)
            project(n + 1, 0, PQ, q_done)
            pe.wait_ge(v_ready, n + 1)
            sum_squares(0, SOFT_PAIRS)
            project(n + 1, 1, PK, k_done)
            stick_values(n, 0)
            stick_tail(n, 1)
            stick_values(n, 1)

            n += 1
            pe.wait_ge(qk_ready, 2 * n + 2)
            stick_z(n, 0)
            pe.wait_ge(root_in, 6)
            project(n, 2, PV, v_done)
            mix(FILLS[0], FILLS[1])
            stick_tail(n, 0)
            turn_v(n)
            stick_z(n, 1)
            mix(FILLS[1], FILLS[2])
            stick_values(n, 0)
            stick_tail(n, 1)
            mix(FILLS[2], FILLS[3])
            stick_values(n, 1)
            mix(FILLS[3], FILLS[4])
            pe.wait_ge(v_ready, PAIRS)
            sum_squares(SOFT_PAIRS, PAIRS)
            mix(FILLS[4], FILLS[5])

            def turn_h2(t):
                pe.wait_ge(h2_ready, t + 1)
                for c in range(KC):
                    if c % 4 == 0 and t:
                        pe.wait_ge(h2T_ready, 2 * t - 1 + c // 4)
                    mm = pe.transpose(S[c // 4][:, (c % 4) * P:(c % 4 + 1) * P], h2_rows[:, t, c * P:(c + 1) * P], ident[:, :])
                    if c % 4 == 3:
                        mm.then_inc(turned2, 1)

            def route(t):
                o = bank[2][:, t * ROUTES:(t + 1) * ROUTES]
                pe.matmul(o, ones[0:1, :], br[:, :], start=True, stop=False)
                for c in range(KC):
                    if c % 4 == 0:
                        pe.wait_ge(h2T_ready, 2 * t + 1 + c // 4)
                    mm = pe.matmul(o, h2T[:, t % 2, c, :], wr[:, c, :], start=False, stop=(c == KC - 1))
                mm.then_inc(routed, 1)

            pe.wait_ge(small_in, 48)
            first = FILLS[-1]
            mix(first, first + 4)
            for t in range(TILES):
                if t + 2 < TILES:
                    mix(first + 2 * t + 4, first + 2 * t + 6)
                turn_h2(t)
                route(t)

            pe.wait_ge(member_ready, 1)
            for t in range(TILES):
                for s in range(t + 1):
                    mm = pe.matmul(bank[3][:, t * EXPERTS:(t + 1) * EXPERTS], (before_b if s == t else ones_b)[:, :], member[:, s, :],
                                   start=(s == 0), stop=(s == t))
            mm.then_inc(ranked, 1)
            for t in range(TILES):
                mm = pe.matmul(bank[4][0:1, 0:EXPERTS], ones_b[:, 0:1], member[:, t, :], start=(t == 0), stop=(t == TILES - 1))
            mm.then_inc(counted, 1)

            pe.wait_ge(hot_ready, 1)
            for n in range(TOPK * TILES):
                for place in (place_low, place_high):
                    mm = pe.matmul(bank[5][:, 0:COLS], slot_hot[:, n, :], place[:, n, :],
                                   start=(n == 0 and place is place_low), stop=(n == TOPK * TILES - 1 and place is place_high))
            mm.then_inc(slots_done, 1)

            XT, GU, AT, Y = bank[0:2], bank[2:4], bank[4], bank[5:7]

            def turn_rows(it, b):
                pe.wait_ge(gathered[b], it * 16 + 16)
                for c in range(KC):
                    if c % 4 == 0 and not (isinstance(it, int) and it + b == 0):
                        pe.wait_ge(xT_ready[c // 4], it * SETS + b)
                    mm = pe.transpose(XT[c // 4][:, (c % 4) * P:(c % 4 + 1) * P], x_slot[b][:, c * P:(c + 1) * P], ident[:, :])
                mm.then_inc(xT_done, 1)

            def gate_up(it, b, part):
                half = part // 2
                w = sets[b][:, 0:KC * 2 * DE].rearrange("p (c f) -> p c f", c=KC)
                if part == 0:
                    pe.wait_ge(gu_in[b], it * 16 + 16)
                    if not (isinstance(it, int) and b < 2):
                        pe.wait_ge(act_ready, it * SETS + b - 1)
                pe.wait_ge(xT_ready[half], it * SETS + b + 1)
                out = GU[b % 2][:, :]
                for c in range(*((0, WHOLE), (WHOLE, 4), (4, KC))[part]):
                    if c < WHOLE:
                        pe.matmul(out, xT[:, b % 2, c, :], w[:, c, :], start=(c == 0), stop=False)
                        continue
                    k = c - WHOLE
                    if k % 2 == 0:
                        pe.wait_ge(gu_ready, it * (SETS * GU_SPLITS) + (b * GU_SPLITS + k // 2 + 1))
                    pe.matmul(out, xT_high[:, b % 2, k, :], gu_high[:, k, :], start=False, stop=False)
                    pe.matmul(out, xT_low[:, b % 2, k, :], gu_high[:, k, :], start=False, stop=False)
                    mm = pe.matmul(out, xT_high[:, b % 2, k, :], gu_low[:, k, :], start=False, stop=(c == KC - 1))
                if half:
                    mm.then_inc(gu_done, 1)

            def turn_act(it, b):
                pe.wait_ge(act_ready, it * SETS + b + 1)
                for c in range(RC):
                    mm = pe.transpose(AT[:, c * P:(c + 1) * P], act_t[:, 3, c * P:(c + 1) * P], ident[:, :])
                mm.then_inc(actT_done, 1)

            def down(it, b):
                w = sets[b][:, KC * 2 * DE:].rearrange("p (c d) -> p c d", c=RC)
                pe.wait_ge(down_in[b], it * 16 + 16)
                pe.wait_ge(actT_ready, it * SETS + b + 1)
                for half in range(2):
                    if not (isinstance(it, int) and it * SETS + b == 0):
                        pe.wait_ge((y0_copied, y1_copied)[half], it * SETS + b)
                    for c in range(RC):
                        mm = pe.matmul(Y[half][:, :], actT[:, b % 2, c, :], w[:, c, half * 512:(half + 1) * 512],
                                       start=(c == 0), stop=(c == RC - 1))
                    mm.then_inc(y_done, 1)

            def expert_step(it, b, first=False):
                before = (it, b - 1) if b else (it - 1, SETS - 1)
                gate_up(it, b, 0)
                if not first:
                    turn_act(*before)
                turn_rows(*((it, b + 1) if b + 1 < SETS else (it + 1, 0)))
                gate_up(it, b, 1)
                gate_up(it, b, 2)
                if not first:
                    down(*before)

            pe.wait_ge(turns_ready, 1)
            turns = pe.value_load(turns_i[0:1, 0:1], min_val=EXPERT_TURNS, max_val=EXPERT_TURNS * SLOT_TURNS)
            last = pe.value_load(turns_i[0:1, 1:2], min_val=EXPERT_TURNS - 1, max_val=EXPERT_TURNS * SLOT_TURNS - 1)
            turn_rows(0, 0)
            for b in range(SETS):
                expert_step(0, b, first=(b == 0))
            with pe.Fori(1, turns) as it:
                for b in range(SETS):
                    expert_step(it, b)
            turn_act(last, SETS - 1)
            down(last, SETS - 1)

        @block.scalar
        def _(act):
            own = Tally(act, act_own)
            act.preload_act_table_set("natural_log_exp_and_others")

            def root(v, r, wait, done):
                wait()
                own.step(act.activation(r, v, ACT.Ln))
                act.activation(r, r, ACT.Exp, scale=-0.5).then_inc(done, 1)

            def split_high(n, w):
                act.wait_ge(w_in[w], n * 16 + 16)
                if w == 2:
                    act.wait_ge(q_done, n + 1)
                elif not isinstance(n, int) or n:
                    act.wait_ge((v_done, k_done)[w], n)
                act.activation(w_split[w][0][:, :, :], w_whole[w], ACT.Copy).then_inc(w_high[w], 1)

            for t in range(TILES + 3):
                if t < TILES:
                    act.wait_ge(x_in[t], 16)
                    act.activation(h_rows[:, t, :], x_rows[:, t, :], ACT.Square, accum_out=ss[:, t:t + 1]).then_inc(squares_done, 1)
                if 1 <= t <= TILES:
                    root(var[:, t - 1:t], rs[:, t - 1:t], lambda: act.wait_ge(root_in, t), root_ready)
                if 2 <= t < TILES + 2:
                    for half in range(2):
                        act.wait_ge(turned, 2 * (t - 2) + half + 1)
                        high, turned_rows = hT_part(0, t - 2, half)
                        act.activation(high, turned_rows, ACT.Copy).then_inc(hT_high, 1)
                if t in (TILES, TILES + 2):
                    split_high(0, (t - TILES) // 2)
            act.wait_ge(count_ready, 1)
            act.activation(log_count[:, 1, :], count, ACT.Ln).then_inc(count_ready, 1)

            def evac_q(n):
                act.wait_ge(q_done, n + 1)
                act.activation(qT, PQ[:, :], ACT.Copy, scale=HD ** -0.5).then_inc(qk_ready, 1)

            def evac_k(n):
                act.wait_ge(k_done, n + 1)
                act.activation(kT, PK[:, :], ACT.Copy).then_inc(qk_ready, 1)

            evac_q(0)
            split_high(0, 2)
            evac_k(0)

            def scale_wo(n):
                if isinstance(n, int):
                    rows = wo[:, n, :]
                else:
                    rows = wo[:, bass.ds(n, 1), :].rearrange("p a d -> p (a d)")
                act.activation(rows, rows, ACT.Copy, scale=gain_m[:, bass.ds(n, 1)]).then_inc(wo_scaled, 1)

            def exponent(n, u):
                a, i = divmod(u, TILES)
                w = (i + 1) * P
                act.wait_ge(biased, n * UNITS + (u + 1))
                act.activation(prob[:, u % 4, 0:w], prob[:, u % 4, 0:w], ACT.Exp, bias=neg_max[:, u:u + 1], scale=-1.0,
                               accum_out=den[:, u:u + 1]).then_inc(exp_done, 1)

            def store_T(n, u):
                a, i = divmod(u, TILES)
                act.wait_ge(prob_turned, n * UNITS + (u + 1))
                act.activation(probT[:, a, 0:i + 1, i * P:(i + 1) * P],
                               T[u % 2][:, 0:(i + 1) * P].rearrange("p (j q) -> p j q", q=P), ACT.Copy).then_inc(probT_ready, 1)

            with act.Fori(0, SOFT_PAIRS) as n:
                for u in range(UNITS):
                    exponent(n, u)
                    if u >= 2:
                        store_T(n, u - 2)
                    if u == 0:
                        split_high(n + 1, 1)
                    if u == 2:
                        split_high(n + 1, 0)
                    if u == 6:
                        act.wait_ge(wo_in, 16)
                        act.wait_ge(small_in, 48)
                        scale_wo(n)
                evac_q(n + 1)
                split_high(n + 1, 2)
                store_T(n, UNITS - 2)
                store_T(n, UNITS - 1)
                evac_k(n + 1)

            def square(n):
                act.wait_ge(o_ready, n + 2)
                if n >= len(squares):
                    act.wait_ge(sq_summed, n + 1 - len(squares))
                act.activation(squares[n % len(squares)], o_all[:, n, :], ACT.Square).then_inc(sq_ready, 1)

            for n in range(SOFT_PAIRS, PAIRS):
                for a in range(2):
                    g = 2 * (n - SOFT_PAIRS) + a
                    for j in reversed(range(TILES)):
                        cols = stick[a][:, SB_AT[j]:SB_AT[j] + SB_W[j]]
                        act.wait_ge(z_done, g * TILES + TILES - j)
                        if g >= 2:
                            act.wait_ge(pv_done, 2 * SOFT_PAIRS + g - 1)
                        own.step(act.activation(cols, bank[j][:, 0:SB_W[j]], ACT.Abs))
                        own.step(act.activation(cols, cols, ACT.Exp, scale=-1.0))
                        act.activation(cols, cols, ACT.Ln, bias=1.0).then_inc(ln_done, 1)
                    for j in reversed(range(TILES)):
                        cols = stick[a][:, SB_AT[j]:SB_AT[j] + SB_W[j]]
                        act.wait_ge(stick_sum, g * TILES + TILES - j)
                        act.activation(cols, bank[j][:, 0:SB_W[j]], ACT.Exp).then_inc(stick_exp, 1)
                    if a == 0 and n == SOFT_PAIRS:
                        split_high(n + 1, 0)
                        split_high(n + 1, 1)
                        for k in range(SOFT_PAIRS):
                            square(k)
                        scale_wo(SOFT_PAIRS)
                        scale_wo(SOFT_PAIRS + 1)
                    if a == 0 and n > SOFT_PAIRS:
                        square(SOFT_PAIRS)
                    if a == 1 and n == SOFT_PAIRS:
                        evac_q(n + 1)
                        split_high(n + 1, 2)
                        evac_k(n + 1)
                        root(mix_var[:, 0:2 * TILES], mix_root[:, 0:2 * TILES], lambda: act.wait_ge(root_in, 6), root_ready)
            square(PAIRS - 1)
            root(mix_var[:, 2 * TILES:], mix_root[:, 2 * TILES:], lambda: act.wait_ge(root_in, 7), root_ready)

            def evac_h2T(t):
                for half in range(2):
                    act.wait_ge(turned2, 2 * t + half + 1)
                    act.activation(h2T[:, t % 2, 4 * half:4 * half + 4, :],
                                   bank[half][:, :].rearrange("p (c s) -> p c s", c=4), ACT.Copy).then_inc(h2T_ready, 1)

            for t in range(TILES):
                act.wait_ge(x1_ready, FILLS[-1] + 2 * t + 2)
                act.activation(h2_rows[:, t, :], x_rows[:, t, :], ACT.Square, accum_out=ss[:, t:t + 1]).then_inc(squares_done, 1)
                root(var[:, t:t + 1], rs[:, t:t + 1], lambda: act.wait_ge(root_in, 8 + t), root_ready)
                if t:
                    evac_h2T(t - 1)
            evac_h2T(TILES - 1)

            act.wait_ge(gate_in, 1)
            for t in range(TILES):
                act.activation(group_exp[:, t, :], logits[:, t, 0:GROUPS], ACT.Exp, bias=gsm[:, 0, t:t + 1],
                               accum_out=gsm[:, 1, t:t + 1]).then_inc(gate_out, 1)
            act.wait_ge(gate_in, 2)
            act.activation(gsm[:, 2, :], gsm[:, 0, :], ACT.Exp).then_inc(gate_out, 1)

            act.wait_ge(turns_ready, 1)
            turns = act.value_load(turns_i[0:1, 0:1], min_val=EXPERT_TURNS, max_val=EXPERT_TURNS * SLOT_TURNS)
            last = act.value_load(turns_i[0:1, 1:2], min_val=EXPERT_TURNS - 1, max_val=EXPERT_TURNS * SLOT_TURNS - 1)

            def evac_xT(it, b):
                act.wait_ge(xT_done, it * SETS + b + 1)
                act.activation(xT[:, b % 2, :, :], xT_chunks(0, WHOLE), ACT.Copy).then_inc(xT_split, 1)
                act.activation(xT_high[:, b % 2, 0:4 - WHOLE, :], xT_chunks(WHOLE, 4), ACT.Copy).then_inc(xT_split, 1)
                act.activation(xT_high[:, b % 2, 4 - WHOLE:, :], xT_chunks(4, KC), ACT.Copy).then_inc(xT_split, 1)

            def split_gu_high(it, b):
                act.wait_ge(gu_in[b], it * 16 + 16)
                if not (isinstance(it, int) and it * SETS + b == 0):
                    act.wait_ge(gu_done, it * SETS + b)
                for k in range(GU_SPLITS):
                    act.activation(gu_high[:, 2 * k:2 * k + 2, :], gu_chunks(b, k), ACT.Copy).then_inc(gu_split, 1)

            def silu_exp(it, b):
                act.wait_ge(gu_done, it * SETS + b + 1)
                if not (isinstance(it, int) and it * SETS + b == 0):
                    act.wait_ge(act_ready, it * SETS + b)
                act.activation(act_t[:, 0, :], bank[2 + b % 2][:, 0:DE], ACT.Exp, scale=-1.0).then_inc(sig_ready, 1)

            def evac_actT(it, b):
                act.wait_ge(actT_done, it * SETS + b + 1)
                act.activation(actT[:, b % 2, :, :], bank[4][:, 0:DE].rearrange("p (c s) -> p c s", c=RC),
                               ACT.Copy).then_inc(actT_ready, 1)

            def evac_y0(it, b):
                act.wait_ge(y_done, it * (2 * SETS) + 2 * b + 1)
                if not isinstance(it, int):
                    act.wait_ge(scattered[b], it * 16)
                act.activation(y_slot[:, b, 0:512], bank[5][:, :], ACT.Copy).then_inc(y0_copied, 1)

            def expert_step(it, b, first=False):
                before = (it, b - 1) if b else (it - 1, SETS - 1)
                if not first:
                    split_gu_high(it, b)
                    evac_actT(*before)
                evac_xT(*((it, b + 1) if b + 1 < SETS else (it + 1, 0)))
                silu_exp(it, b)
                if not first:
                    evac_y0(*before)

            split_gu_high(0, 0)
            evac_xT(0, 0)
            for b in range(SETS):
                expert_step(0, b, first=(b == 0))
            with act.Fori(1, turns) as it:
                for b in range(SETS):
                    expert_step(it, b)
            evac_actT(last, SETS - 1)
            evac_y0(last, SETS - 1)

            own = Tally(act, act_end)

            def square_x(t):
                act.wait_ge(x2_ready, TOPK * (t + 1))
                act.activation(h2_rows[:, t, :], x_rows[:, t, :], ACT.Square, accum_out=ss[:, t:t + 1]).then_inc(sq2_done, 1)

            def last_root(t):
                root(var[:, t:t + 1], rs[:, t:t + 1], lambda: act.wait_ge(root_in, 12 + t), root_ready)

            def scale_x(t):
                act.wait_ge(refined, t + 1)
                act.activation(h2_rows[:, t, :], x_rows[:, t, :], ACT.Copy, scale=rs[:, t:t + 1]).then_inc(scaled, 1)

            square_x(0)
            square_x(1)
            last_root(0)
            last_root(1)
            scale_x(0)
            square_x(2)
            scale_x(1)
            last_root(2)
            square_x(3)
            last_root(3)

        @block.vector
        def _(dve):
            own = Tally(dve, dve_own)
            roots = [0]

            def variance(v, total, n):
                dve.tensor_scalar(v, total, 1.0 / n, EPS, ALU.mult, ALU.add).then_inc(root_in, 1)

            def refine(v, r, tmp):
                roots[0] += 1
                dve.wait_ge(root_ready, roots[0])
                own.step(dve.tensor_tensor(tmp, r, r, ALU.mult))
                own.step(dve.tensor_tensor(tmp, tmp, v, ALU.mult))
                own.step(dve.tensor_scalar(tmp, tmp, -0.5, 1.5, ALU.mult, ALU.add))
                own.step(dve.tensor_tensor(r, r, tmp, ALU.mult))

            def split_low(n, w):
                high, low = w_split[w]
                dve.wait_ge(w_high[w], n + 1)
                dve.tensor_tensor(low[:, :, :], w_whole[w], high[:, :, :].bitcast(F32), ALU.subtract).then_inc(w_low[w], 1)

            dve.wait_ge(gain_in, 16)
            for t in range(TILES + 3):
                if t < TILES:
                    dve.wait_ge(squares_done, t + 1)
                    variance(var[:, t:t + 1], ss[:, t:t + 1], D)
                if 1 <= t <= TILES:
                    dve.wait_ge(root_in, t)
                    refine(var[:, t - 1:t], rs[:, t - 1:t], nt[:, t - 1:t])
                    dve.scalar_tensor_tensor(out=h_rows[:, t - 1, :], in0=x_rows[:, t - 1, :], scalar=rs[:, t - 1:t], in1=gain_row[:, :],
                                             op0=ALU.mult, op1=ALU.mult).then_inc(rows_ready, 1)
                if 2 <= t < TILES + 2:
                    for half in range(2):
                        dve.wait_ge(hT_high, 2 * (t - 2) + half + 1)
                        (high, turned_rows), (low, _) = hT_part(0, t - 2, half), hT_part(1, t - 2, half)
                        dve.tensor_tensor(low, turned_rows, high.bitcast(F32), ALU.subtract).then_inc(hT_ready, 1)
                if t in (TILES, TILES + 2):
                    split_low(0, (t - TILES) // 2)
            dve.wait_ge(iota_ready, 5 + len(SLOPES))
            own.step(dve.tensor_scalar(count, neg_dist, float(-P), None, ALU.is_ge))
            for dilation in (4, 16):
                own.step(dve.tensor_scalar(mod_i, dist_i, dilation - 1, None, ALU.bitwise_and))
                own.step(dve.scalar_tensor_tensor(out=count, in0=mod_i, scalar=0.0, in1=count, op0=ALU.is_equal, op1=ALU.add))
            own.step(dve.tensor_scalar(hits, count, 0.0, NEG, ALU.is_equal, ALU.mult))
            dve.tensor_scalar(count, count, 1.0, None, ALU.max).then_inc(count_ready, 1)
            dve.wait_ge(count_ready, 2)
            dve.tensor_tensor(log_count[:, 1, :], log_count[:, 1, :], hits, ALU.add).then_inc(log_ready, 1)
            split_low(0, 2)
            dve.wait_ge(log_ready, 3)
            dve.sem_inc(o_ready, 1)

            def evac_vT(n):
                dve.wait_ge(v_done, n + 1)
                dve.tensor_copy(vT[:, :], PV[:, :]).then_inc(vT_ready, 1)

            def evac_v(n):
                dve.wait_ge(v_turned, n + 1)
                dve.tensor_copy(v_tok[:, :, :], PV[:, :].rearrange("p (j d) -> p j d", j=TILES)).then_inc(v_ready, 1)

            def bias_scores(n, u):
                a, i = divmod(u, TILES)
                w = (i + 1) * P
                dve.wait_ge(score_done, n * UNITS + (u + 1))
                dve.memset(dve_tick[:, u:u + 1], 0.0)
                dve.tensor_tensor_reduce(out=prob[:, u % 4, 0:w], in0=S[u % 2][:, 0:w], in1=bias[:, a, SEQ - w:SEQ],
                                         scale=-1.0, scalar=3e38, op0=ALU.add, op1=ALU.min,
                                         accum_out=neg_max[:, u:u + 1]).then_inc(biased, 1)

            def normalise(n, u):
                a, i = divmod(u, TILES)
                w = (i + 1) * P
                dve.wait_ge(exp_done, n * UNITS + (u + 1))
                own.step(dve.reciprocal(rden[:, u:u + 1], den[:, u:u + 1]))
                dve.tensor_scalar(prob[:, u % 4, 0:w], prob[:, u % 4, 0:w], rden[:, u:u + 1], None, ALU.mult).then_inc(normed, 1)

            def evac_o(n):
                dve.wait_ge(pv_done, 2 * n + 2)
                if isinstance(n, int):
                    dst = o_all[:, n, :]
                else:
                    dst = o_all[:, bass.ds(n, 1), :].rearrange("p a t -> p (a t)")
                dve.tensor_copy(dst, O_BANK[:, :]).then_inc(o_ready, 1)

            with dve.Fori(0, SOFT_PAIRS) as n:
                own.enter(n, 2 + UNITS)
                for a in range(2):
                    own.mark(dve.scalar_tensor_tensor(
                        out=bias[:, a, :], in0=neg_dist, scalar=slope[:, bass.ds(2 * n + a, 1)],
                        in1=log_count[:, bass.ds((n + 2) // 4, 1), :].rearrange("p a t -> p (a t)"),
                        op0=ALU.mult, op1=ALU.add))
                own.wait()
                for u in range(UNITS):
                    bias_scores(n, u)
                    if u == 2:
                        evac_vT(n)
                    if u == 4:
                        evac_v(n)
                    if u >= 1:
                        normalise(n, u - 1)
                    if u == 1:
                        split_low(n + 1, 1)
                    if u == 3:
                        split_low(n + 1, 0)
                normalise(n, UNITS - 1)
                split_low(n + 1, 2)
                evac_o(n)
            own.leave(SOFT_PAIRS)

            def add_mixed(first, end):
                for m in range(first, end):
                    g, t, half = MIX_STEPS[m]
                    cols = x_rows[:, t, half * 512:(half + 1) * 512]
                    dve.wait_ge(mixed, m + 1)
                    if m >= 2 * TILES:
                        dve.wait_ge(x1_ready, m + 1 - 2 * TILES)
                    dve.scalar_tensor_tensor(out=cols, in0=bank[MIX_BANKS[m]][:, :], scalar=mix_root[:, g * TILES + t:g * TILES + t + 1],
                                             in1=cols, op0=ALU.mult, op1=ALU.add).then_inc(x1_ready, 1)

            for n in range(SOFT_PAIRS, PAIRS):
                for a in range(2):
                    g = 2 * (n - SOFT_PAIRS) + a
                    for j in reversed(range(TILES)):
                        cols = slice(SB_AT[j], SB_AT[j] + SB_W[j])
                        dve.wait_ge(ln_done, g * TILES + TILES - j)
                        own.step(dve.scalar_tensor_tensor(out=soft[a][:, cols], in0=bank[j][:, 0:SB_W[j]], scalar=0.0,
                                                          in1=stick[a][:, cols], op0=ALU.max, op1=ALU.add))
                        diag = soft[a][:, SB_AT[j]:SB_AT[j] + P]
                        dve.tensor_tensor(diag, diag, before[:, :], ALU.mult).then_inc(soft_ready, 1)
                    if a == 0:
                        evac_vT(n)
                        if n + 1 < PAIRS:
                            evac_v(n)
                            split_low(n + 1, 0)
                            split_low(n + 1, 1)
                        else:
                            add_mixed(FILLS[0], FILLS[1])
                            evac_v(n)
                if n == SOFT_PAIRS:
                    split_low(n + 1, 2)
                    dve.wait_ge(sq_summed, SOFT_PAIRS)
                    for g, (lo, hi) in enumerate(MIX_GROUPS[0:2]):
                        cols = slice(g * TILES, (g + 1) * TILES)
                        variance(mix_var[:, cols], PV[:, cols], (hi - lo) * P)
                    dve.wait_ge(root_in, 6)
                    refine(mix_var[:, 0:2 * TILES], mix_root[:, 0:2 * TILES], mix_tmp[:, 0:2 * TILES])
                    evac_o(n)
            add_mixed(FILLS[1], FILLS[3])
            evac_o(PAIRS - 1)
            add_mixed(FILLS[3], FILLS[4] + 1)
            dve.wait_ge(sq_summed, PAIRS)
            cols = slice(2 * TILES, 3 * TILES)
            variance(mix_var[:, cols], PV[:, cols], (PAIRS - SOFT_PAIRS) * P)
            dve.wait_ge(root_in, 7)
            refine(mix_var[:, cols], mix_root[:, cols], mix_tmp[:, cols])
            add_mixed(FILLS[4] + 1, FILLS[5])

            for t in range(TILES):
                add_mixed(FILLS[-1] + 2 * t, FILLS[-1] + 2 * t + 2)
                dve.wait_ge(squares_done, TILES + t + 1)
                variance(var[:, t:t + 1], ss[:, t:t + 1], D)
                dve.wait_ge(root_in, 8 + t)
                refine(var[:, t:t + 1], rs[:, t:t + 1], nt[:, t:t + 1])
                dve.wait_ge(gain_in, 32)
                dve.scalar_tensor_tensor(out=h2_rows[:, t, :], in0=x_rows[:, t, :], scalar=rs[:, t:t + 1], in1=gain_row[:, :],
                                         op0=ALU.mult, op1=ALU.mult).then_inc(h2_ready, 1)

            def best(lo):
                for t in range(lo, lo + TILES):
                    own.mark(dve.max(out=top[:, t, :], in_=pad[:, t, :]))
                own.wait()
                for t in range(lo, lo + TILES):
                    own.mark(dve.max_index(out=top_i[:, t, :], in_max=top[:, t, :], in_values=pad[:, t, :]))
                own.wait()
                own.step(dve.tensor_copy(idx_f[:, lo:lo + TILES, :], top_i[:, lo:lo + TILES, 0:2]))

            dve.wait_ge(routed, TILES)
            dve.wait_ge(consts_ready, 4)
            own.mark(dve.tensor_copy(logits[:, :, :], bank[2][:, 0:TILES * ROUTES].rearrange("p (t n) -> p t n", t=TILES)))
            own.step(dve.tensor_copy(pad[:, 0:TILES, 0:GROUPS],
                                     bank[2][:, 0:TILES * ROUTES].rearrange("p (t n) -> p t n", t=TILES)[:, :, 0:GROUPS]))
            best(0)
            dve.tensor_scalar(gsm[:, 0, :], top[:, 0:TILES, 0], -1.0, None, ALU.mult).then_inc(gate_in, 1)
            own.step(dve.tensor_tensor(pick[:, :, :], iota[:, 0:GROUPS].unsqueeze(1).to_broadcast([P, TILES, GROUPS]),
                                       idx_f[:, 0:TILES, 0:1].to_broadcast([P, TILES, GROUPS]), ALU.is_equal))
            for t in range(TILES):
                own.mark(dve.tensor_tensor(scr[:, t, :].rearrange("p (g e) -> p g e", g=GROUPS),
                                           logits[:, t, GROUPS:].rearrange("p (g e) -> p g e", g=GROUPS),
                                           pick[:, t, :].unsqueeze(2).to_broadcast([P, GROUPS, PER_GROUP]), ALU.mult))
            own.wait()
            own.step(dve.tensor_reduce(pad[:, TILES:2 * TILES, 0:PER_GROUP], scr[:, :, :].rearrange("p t (g e) -> p t e g", g=GROUPS),
                                       mybir.AxisListType.X, ALU.add))
            best(TILES)
            dve.wait_ge(gate_out, TILES)
            own.step(dve.reciprocal(gsm[:, 3, :], gsm[:, 1, :]))
            dve.tensor_tensor(gsm[:, 0, :], top[:, TILES:2 * TILES, 1], top[:, TILES:2 * TILES, 0], ALU.subtract).then_inc(gate_in, 1)
            for k in range(TOPK):
                own.mark(dve.scalar_tensor_tensor(out=eid[:, k, :], in0=idx_f[:, 0:TILES, 0], scalar=float(PER_GROUP),
                                                  in1=idx_f[:, TILES:2 * TILES, k], op0=ALU.mult, op1=ALU.add))
            own.wait()
            for k in range(TOPK):
                own.mark(dve.tensor_tensor(chosen[:, k, :, :], iota[:, 0:EXPERTS].unsqueeze(1).to_broadcast([P, TILES, EXPERTS]),
                                           eid[:, k, :].unsqueeze(2).to_broadcast([P, TILES, EXPERTS]), ALU.is_equal))
            own.wait()
            dve.tensor_tensor(member[:, :, :], chosen[:, 0, :, :], chosen[:, 1, :, :], ALU.add).then_inc(member_ready, 1)
            dve.wait_ge(gate_out, TILES + 1)
            own.step(dve.tensor_scalar(gsm[:, 1, :], gsm[:, 2, :], 1.0, None, ALU.add))
            own.step(dve.reciprocal(gsm[:, 1, :], gsm[:, 1, :]))
            own.step(dve.tensor_tensor(weight[:, 0, :], gsm[:, 1, :], gsm[:, 3, :], ALU.mult))
            own.step(dve.tensor_tensor(weight[:, 1, :], weight[:, 0, :], gsm[:, 2, :], ALU.mult))
            dve.wait_ge(ranked, 1)
            for k in range(TOPK):
                own.step(dve.tensor_tensor(scr[:, :, :], bank[3][:, 0:TILES * EXPERTS].rearrange("p (t e) -> p t e", t=TILES),
                                           chosen[:, k, :, :], ALU.mult))
                own.step(dve.tensor_reduce(rank[:, k, :], scr[:, :, :], mybir.AxisListType.X, ALU.add))
            own.step(dve.tensor_scalar(turn_f[:, :, :], rank[:, :, :], float(P), None, ALU.is_ge))
            for c in range(2, SLOT_TURNS):
                own.step(dve.scalar_tensor_tensor(out=turn_f[:, :, :], in0=rank[:, :, :], scalar=float(c * P), in1=turn_f[:, :, :],
                                                  op0=ALU.is_ge, op1=ALU.add))
            own.mark(dve.scalar_tensor_tensor(out=slot_f[:, :, :], in0=turn_f[:, :, :], scalar=-float(P), in1=rank[:, :, :],
                                              op0=ALU.mult, op1=ALU.add))
            own.step(dve.scalar_tensor_tensor(out=tmp_f[:, :, :], in0=turn_f[:, :, :], scalar=float(EXPERTS), in1=eid[:, :, :],
                                              op0=ALU.mult, op1=ALU.add))
            def hot(out, values, width):
                return dve.tensor_tensor(out, iota[:, 0:width].unsqueeze(1).to_broadcast([P, TOPK * TILES, width]),
                                         per_token(values, width), ALU.is_equal)

            def per_token(values, width):
                return values[:, :, :].rearrange("p k t -> p (k t)").unsqueeze(2).to_broadcast([P, TOPK * TILES, width])

            own.step(hot(place_hot, tmp_f, COLS))
            own.mark(dve.tensor_tensor(place_low, place_hot, per_token(token_low, COLS), ALU.mult))
            own.mark(dve.tensor_tensor(place_high, place_hot, per_token(token_high, COLS), ALU.mult))
            own.mark(hot(slot_hot, slot_f, P))
            own.wait()
            dve.sem_inc(hot_ready, 1)
            dve.wait_ge(counted, 1)
            own.step(dve.tensor_reduce(fullest[:, 0:1], bank[4][0:1, 0:EXPERTS], mybir.AxisListType.X, ALU.max))
            own.step(dve.tensor_scalar(turns_i[:, 0:1], fullest[:, 0:1], float(P - 1), None, ALU.add))
            own.step(dve.tensor_scalar(turns_i[:, 0:1], turns_i[:, 0:1], 7, 2, ALU.logical_shift_right, ALU.logical_shift_left))
            dve.tensor_scalar(turns_i[:, 1:2], turns_i[:, 0:1], 1, None, ALU.subtract).then_inc(turns_ready, 1)
            dve.wait_ge(slots_done, 1)
            own.step(dve.tensor_scalar(taken[:, :], bank[5][:, 0:COLS], 0.0, 2.0 * BIG, ALU.is_equal, ALU.mult))
            own.step(dve.scalar_tensor_tensor(out=slot_to[:, 0:COLS], in0=bank[5][:, 0:COLS], scalar=-1.0, in1=taken[:, :],
                                              op0=ALU.add, op1=ALU.add))
            dve.tensor_scalar(slot_of[:, :], slot_to[:, :], 1, None, ALU.logical_shift_right).then_inc(slots_ready, 1)

            dve.wait_ge(turns_ready, 1)
            turns = dve.value_load(turns_i[0:1, 0:1], min_val=EXPERT_TURNS, max_val=EXPERT_TURNS * SLOT_TURNS)
            last = dve.value_load(turns_i[0:1, 1:2], min_val=EXPERT_TURNS - 1, max_val=EXPERT_TURNS * SLOT_TURNS - 1)

            def swiglu(it, b):
                gu = bank[2 + b % 2]
                dve.wait_ge(sig_ready, it * SETS + b + 1)
                own.step(dve.tensor_scalar(act_t[:, 1, :], act_t[:, 0, :], 1.0, None, ALU.add))
                own.step(dve.reciprocal(act_t[:, 1, :], act_t[:, 1, :]))
                own.step(dve.tensor_tensor(act_t[:, 2, :], gu[:, 0:DE], act_t[:, 1, :], ALU.mult))
                dve.tensor_tensor(act_t[:, 3, :], gu[:, DE:2 * DE], act_t[:, 2, :], ALU.mult).then_inc(act_ready, 1)

            def split_gu_low(it, b):
                for k in range(GU_SPLITS):
                    dve.wait_ge(gu_split, it * (SETS * GU_SPLITS) + (b * GU_SPLITS + k + 1))
                    dve.tensor_tensor(gu_low[:, 2 * k:2 * k + 2, :], gu_chunks(b, k), gu_high[:, 2 * k:2 * k + 2, :].bitcast(F32),
                                      ALU.subtract).then_inc(gu_ready, 1)

            def split_xT_low(it, b):
                for half, (lo, hi) in enumerate(((WHOLE, 4), (4, KC))):
                    dve.wait_ge(xT_split, it * (3 * SETS) + (3 * b + 2 + half))
                    dve.tensor_tensor(xT_low[:, b % 2, lo - WHOLE:hi - WHOLE, :], xT_chunks(lo, hi),
                                      xT_high[:, b % 2, lo - WHOLE:hi - WHOLE, :].bitcast(F32), ALU.subtract).then_inc(xT_ready[half], 1)

            def evac_y1(it, b):
                dve.wait_ge(y_done, it * (2 * SETS) + 2 * b + 2)
                if not isinstance(it, int):
                    dve.wait_ge(scattered[b], it * 16)
                dve.tensor_copy(y_slot[:, b, 512:1024], bank[6][:, :]).then_inc(y1_copied, 1)

            def expert_step(it, b, first=False):
                if not first:
                    split_gu_low(it, b)
                split_xT_low(*((it, b + 1) if b + 1 < SETS else (it + 1, 0)))
                swiglu(it, b)
                if not first:
                    evac_y1(*((it, b - 1) if b else (it - 1, SETS - 1)))

            split_gu_low(0, 0)
            split_xT_low(0, 0)
            for b in range(SETS):
                expert_step(0, b, first=(b == 0))
            with dve.Fori(1, turns) as it:
                own.enter(it - 1, 3 * SETS)
                for b in range(SETS):
                    expert_step(it, b)
            evac_y1(last, SETS - 1)

            own = Tally(dve, end_own)

            def combine(t, k):
                if k == 0:
                    dve.wait_ge(y_in[t], 16)
                dve.scalar_tensor_tensor(out=x_rows[:, t, :], in0=y_pairs[t][:, k * D:(k + 1) * D],
                                         scalar=weight[:, k, t:t + 1], in1=x_rows[:, t, :], op0=ALU.mult,
                                         op1=ALU.add).then_inc(x2_ready, 1)
                dve.wait_ge(x2_ready, TOPK * t + k + 1)

            def last_variance(t):
                dve.wait_ge(sq2_done, t + 1)
                variance(var[:, t:t + 1], ss[:, t:t + 1], D)

            def last_refine(t):
                dve.wait_ge(root_in, 12 + t)
                refine(var[:, t:t + 1], rs[:, t:t + 1], nt[:, t:t + 1])
                if t < 2:
                    dve.sem_inc(refined, 1)

            def finish(t):
                dve.scalar_tensor_tensor(out=h2_rows[:, t, :], in0=x_rows[:, t, :], scalar=rs[:, t:t + 1], in1=gain_row[:, :],
                                         op0=ALU.mult, op1=ALU.mult).then_inc(out_ready[t], 1)

            dve.wait_ge(gain_in, 48)
            for t in range(2):
                combine(t, 0)
                combine(t, 1)
            last_variance(0)
            combine(2, 0)
            last_variance(1)
            last_refine(0)
            combine(2, 1)
            last_refine(1)
            combine(3, 0)
            last_variance(2)
            combine(3, 1)
            last_refine(2)
            finish(2)
            last_variance(3)
            last_refine(3)
            finish(3)


def kernel(x, ln1_g, w_in, mix_norm_g, w_out, ln2_g, w_group_router, b_group_router, w_expert_router,
           b_expert_router, w_gate, w_up, w_down, final_norm_g):
    import numpy as np
    import concourse.bacc as bacc
    from concourse.bass_utils import run_bass_kernel_spmd

    heads = [*range(0, 4), *range(8, 16), *range(4, 8)]
    cont = np.ascontiguousarray
    wi = np.asarray(w_in)[0].reshape(KC, P, 3, HEADS, HD)[:, :, [1, 0, 2]][:, :, :, heads].reshape(KC, P, 3, PAIRS, P)
    gate, up = (np.asarray(w)[0].reshape(EXPERTS, KC, P, DE) for w in (w_gate, w_up))
    gu = np.concatenate([gate, up], axis=-1).transpose(0, 2, 1, 3).reshape(EXPERTS, P, KC * 2 * DE)
    down = np.asarray(w_down)[0].reshape(EXPERTS, RC, P, D).transpose(0, 2, 1, 3).reshape(EXPERTS, P, RC * D)
    route = np.concatenate([np.asarray(w_group_router)[0],
                            np.asarray(w_expert_router)[0].transpose(1, 0, 2).reshape(D, EXPERTS)], axis=-1)
    arrays = {
        "x": cont(np.asarray(x)[0]),
        "gain1": cont(np.asarray(ln1_g)[0]),
        "w_qkv": cont(wi.transpose(3, 1, 2, 0, 4).reshape(PAIRS, P, 3 * KC * P)),
        "gain_mix": cont(np.asarray(mix_norm_g)[0].reshape(HEADS, HD)[heads].reshape(PAIRS, P).T),
        "w_out": cont(np.asarray(w_out)[0].reshape(HEADS, HD, D)[heads].reshape(PAIRS, P, D).transpose(1, 0, 2).reshape(P, PAIRS * D)),
        "gain2": cont(np.asarray(ln2_g)[0]),
        "w_route": cont(route.reshape(KC, P, ROUTES).transpose(1, 0, 2).reshape(P, KC * ROUTES)),
        "b_route": cont(np.concatenate([np.asarray(b_group_router)[0], np.asarray(b_expert_router)[0].reshape(EXPERTS)])[None]),
        "w_expert": cont(np.concatenate([gu, down], axis=-1)),
        "gain_final": cont(np.asarray(final_norm_g)),
    }
    nc = bacc.Bacc("TRN2", target_bir_lowering=False, num_devices=1)
    args = [nc.dram_tensor(n, a.shape, mybir.dt.float32, kind="ExternalInput").ap() for n, a in arrays.items()]
    out = nc.dram_tensor("out", (SEQ, D), mybir.dt.float32, kind="ExternalOutput").ap()
    decoder_layer(nc, *args, out)
    r = run_bass_kernel_spmd(nc, [arrays], core_ids=[0])
    return r.results[0]["out"].reshape(1, SEQ, D)
```
